# Optimizing a Trainium2 kernel written in Bass

```python
import math
import jax, jax.numpy as jnp
from jax import lax
import numpy as np

D_MODEL = 2048
BATCH = 1
SEQ = 256
DEPTH = 1

CONV_DIM = D_MODEL
CONV_WIDTH = 3
GDN_K_HEADS = 16
GDN_V_HEADS = 32
GDN_K_DIM = D_MODEL // GDN_K_HEADS
GDN_V_DIM = D_MODEL // GDN_V_HEADS
GDN_QK_WIDTH = GDN_K_HEADS * GDN_K_DIM
GDN_V_WIDTH = GDN_V_HEADS * GDN_V_DIM
GDN_CONV_WIDTH = 4
GDN_CHUNK = 64
FOX_HEADS = 16
FOX_DIM = D_MODEL // FOX_HEADS
FOX_WIDTH = FOX_HEADS * FOX_DIM
Q_BLOCK = 128
D_FF = 4 * D_MODEL
LN_EPS = 1e-5
NORM_EPS = 1e-6
DEEPNORM_ALPHA = (2 * DEPTH) ** 0.25
DEEPNORM_BETA = (8 * DEPTH) ** -0.25
SPLIT_SIZES = (CONV_DIM, CONV_DIM, CONV_DIM,
               GDN_QK_WIDTH, GDN_QK_WIDTH, GDN_V_WIDTH, GDN_V_WIDTH,
               GDN_V_HEADS, GDN_V_HEADS,
               FOX_WIDTH, FOX_WIDTH, FOX_WIDTH, FOX_HEADS,
               D_MODEL, D_MODEL, D_MODEL)
IN_WIDTH = sum(SPLIT_SIZES)

kernel_name = 'hybrid_conv_gdn_fox_gated_merge_deepnorm_adaln'

def layer_norm(x, g, b):
    xf = x.astype(jnp.float32)
    mu = jnp.mean(xf, axis=-1, keepdims=True)
    var = jnp.mean(jnp.square(xf - mu), axis=-1, keepdims=True)
    return ((xf - mu) * lax.rsqrt(var + LN_EPS) * g + b).astype(x.dtype)

def causal_depthwise_conv(x, w):
    width = w.shape[0]
    seq = x.shape[1]
    xp = jnp.pad(x, ((0, 0), (width - 1, 0), (0, 0)))
    out = xp[:, 0:seq] * w[0]
    for i in range(1, width):
        out = out + xp[:, i:i + seq] * w[i]
    return out

def l2_normalize(t):
    tf = t.astype(jnp.float32)
    return tf * lax.rsqrt(jnp.sum(tf * tf, axis=-1, keepdims=True) + NORM_EPS)

def short_conv_branch(b_gate, c_gate, h, conv_w):
    return b_gate * causal_depthwise_conv(c_gate * h, conv_w)

def chunked_gated_delta_rule(q, k, v, beta, g):
    bsz, seq, heads, dk = q.shape
    dv = v.shape[-1]
    n_chunks = seq // GDN_CHUNK

    def chunks(t):
        t = t.reshape((bsz, n_chunks, GDN_CHUNK, heads) + t.shape[3:])
        return jnp.moveaxis(t, 3, 1)

    q = chunks(q) * (dk ** -0.5)
    k = chunks(k)
    v = chunks(v)
    beta = chunks(beta)
    g = jnp.cumsum(chunks(g), axis=-1)
    tril = jnp.tril(jnp.ones((GDN_CHUNK, GDN_CHUNK), dtype=bool))
    strict = jnp.tril(jnp.ones((GDN_CHUNK, GDN_CHUNK), dtype=bool), k=-1)
    decay = jnp.exp(jnp.where(tril, g[..., :, None] - g[..., None, :], -jnp.inf))
    k_beta = k * beta[..., None]
    lower = jnp.where(strict, jnp.einsum('bhncd,bhnsd->bhncs', k_beta, k) * decay, 0.0)
    eye = jnp.eye(GDN_CHUNK, dtype=lower.dtype)
    rhs = jnp.concatenate([v * beta[..., None], k_beta * jnp.exp(g)[..., None]], axis=-1)
    sol = lax.linalg.triangular_solve(lower + eye, rhs, left_side=True, lower=True, unit_diagonal=True)
    u = sol[..., :dv]
    w = sol[..., dv:]
    intra = jnp.where(tril, jnp.einsum('bhncd,bhnsd->bhncs', q, k) * decay, 0.0)
    q_decay = q * jnp.exp(g)[..., None]
    k_state = k * jnp.exp(g[..., -1:] - g)[..., None]
    chunk_decay = jnp.exp(g[..., -1])

    def step(state, xs):
        u_i, w_i, qd_i, intra_i, ks_i, cd_i = xs
        v_new = u_i - jnp.einsum('bhck,bhkv->bhcv', w_i, state)
        o_i = jnp.einsum('bhck,bhkv->bhcv', qd_i, state) + jnp.einsum('bhcs,bhsv->bhcv', intra_i, v_new)
        state = state * cd_i[..., None, None] + jnp.einsum('bhck,bhcv->bhkv', ks_i, v_new)
        return state, o_i

    xs = tuple(jnp.moveaxis(t, 2, 0) for t in (u, w, q_decay, intra, k_state, chunk_decay))
    state0 = jnp.zeros((bsz, heads, dk, dv), jnp.float32)
    _, o = lax.scan(step, state0, xs)
    return jnp.transpose(o, (1, 0, 3, 2, 4)).reshape(bsz, seq, heads, dv)

def gated_deltanet_branch(q, k, v, z, b_logit, a_logit, conv_w, a_log, dt_bias, norm_w):
    bsz, seq, _ = q.shape
    qkv = jax.nn.silu(causal_depthwise_conv(jnp.concatenate([q, k, v], axis=-1), conv_w))
    q, k, v = jnp.split(qkv, [GDN_QK_WIDTH, 2 * GDN_QK_WIDTH], axis=-1)
    rep = GDN_V_HEADS // GDN_K_HEADS
    q = jnp.repeat(l2_normalize(q.reshape(bsz, seq, GDN_K_HEADS, GDN_K_DIM)), rep, axis=2)
    k = jnp.repeat(l2_normalize(k.reshape(bsz, seq, GDN_K_HEADS, GDN_K_DIM)), rep, axis=2)
    v = v.reshape(bsz, seq, GDN_V_HEADS, GDN_V_DIM).astype(jnp.float32)
    beta = jax.nn.sigmoid(b_logit.astype(jnp.float32))
    g = -jnp.exp(a_log.astype(jnp.float32)) * jax.nn.softplus(a_logit.astype(jnp.float32) + dt_bias.astype(jnp.float32))
    o = chunked_gated_delta_rule(q, k, v, beta, g)
    o = o * lax.rsqrt(jnp.mean(o * o, axis=-1, keepdims=True) + NORM_EPS) * norm_w
    o = o * jax.nn.silu(z.reshape(bsz, seq, GDN_V_HEADS, GDN_V_DIM).astype(jnp.float32))
    return o.reshape(bsz, seq, GDN_V_WIDTH).astype(z.dtype)

def forgetting_attention_branch(q, k, v, f_logit, f_bias):
    bsz, seq, _ = q.shape

    def heads(t):
        return t.reshape(bsz, seq, FOX_HEADS, FOX_DIM).transpose(0, 2, 1, 3)

    q, k, v = heads(q), heads(k), heads(v)
    log_f = jax.nn.log_sigmoid(f_logit.astype(jnp.float32) + f_bias.astype(jnp.float32))
    cum = jnp.cumsum(log_f, axis=1).transpose(0, 2, 1)
    scale = FOX_DIM ** -0.5
    outs = []
    for blk in range(seq // Q_BLOCK):
        q0, q1 = blk * Q_BLOCK, (blk + 1) * Q_BLOCK
        s = jnp.einsum('bhqd,bhkd->bhqk', q[:, :, q0:q1], k[:, :, :q1],
                       preferred_element_type=jnp.float32) * scale
        s = s + cum[:, :, q0:q1, None] - cum[:, :, None, :q1]
        causal = (q0 + jnp.arange(Q_BLOCK))[:, None] >= jnp.arange(q1)[None, :]
        p = jax.nn.softmax(jnp.where(causal, s, -jnp.inf), axis=-1)
        outs.append(jnp.einsum('bhqk,bhkd->bhqd', p.astype(v.dtype), v[:, :, :q1]))
    o = jnp.concatenate(outs, axis=2)
    return o.transpose(0, 2, 1, 3).reshape(bsz, seq, FOX_WIDTH)

def setup_inputs(seed: int = 0) -> dict:
    key = jax.random.key(seed)
    ks = jax.random.split(key, 24)
    f32 = jnp.float32

    def nrm(k, shape, scale):
        return jax.random.normal(k, shape, f32) * scale

    x = nrm(ks[0], (BATCH, SEQ, D_MODEL), 1.0)
    c = nrm(ks[1], (BATCH, D_MODEL), 1.0)
    w_ada = nrm(ks[2], (DEPTH, D_MODEL, 6 * D_MODEL), 0.5 * D_MODEL ** -0.5)
    b_ada = nrm(ks[3], (DEPTH, 6 * D_MODEL), 0.02)
    w_in = nrm(ks[4], (DEPTH, D_MODEL, IN_WIDTH), D_MODEL ** -0.5)
    conv_w = nrm(ks[5], (DEPTH, CONV_WIDTH, CONV_DIM), CONV_WIDTH ** -0.5)
    gdn_conv_w = nrm(ks[6], (DEPTH, GDN_CONV_WIDTH, 2 * GDN_QK_WIDTH + GDN_V_WIDTH), GDN_CONV_WIDTH ** -0.5)
    gdn_a_log = jnp.log(jax.random.uniform(ks[7], (DEPTH, GDN_V_HEADS), f32, 1.0, 16.0))
    dt = jnp.exp(jax.random.uniform(ks[8], (DEPTH, GDN_V_HEADS), f32, math.log(1e-3), math.log(1e-1)))
    gdn_dt_bias = dt + jnp.log(-jnp.expm1(-dt))
    gdn_norm_w = 1.0 + nrm(ks[9], (DEPTH, GDN_V_DIM), 0.02)
    fox_f_bias = jax.random.uniform(ks[10], (DEPTH, FOX_HEADS), f32, 1.0, 4.0)
    w_branch_a = nrm(ks[11], (DEPTH, CONV_DIM, D_MODEL), DEEPNORM_BETA * CONV_DIM ** -0.5)
    w_branch_b = nrm(ks[12], (DEPTH, GDN_V_WIDTH, D_MODEL), DEEPNORM_BETA * GDN_V_WIDTH ** -0.5)
    w_branch_c = nrm(ks[13], (DEPTH, FOX_WIDTH, D_MODEL), DEEPNORM_BETA * FOX_WIDTH ** -0.5)
    w_o = nrm(ks[14], (DEPTH, D_MODEL, D_MODEL), DEEPNORM_BETA * D_MODEL ** -0.5)
    ln1_g = 1.0 + nrm(ks[15], (DEPTH, D_MODEL), 0.02)
    ln1_b = nrm(ks[16], (DEPTH, D_MODEL), 0.02)
    w_ff1 = nrm(ks[17], (DEPTH, D_MODEL, D_FF), D_MODEL ** -0.5)
    w_ff2 = nrm(ks[18], (DEPTH, D_FF, D_MODEL), DEEPNORM_BETA * D_FF ** -0.5)
    ln2_g = 1.0 + nrm(ks[19], (DEPTH, D_MODEL), 0.02)
    ln2_b = nrm(ks[20], (DEPTH, D_MODEL), 0.02)
    return {'x': x, 'c': c, 'w_ada': w_ada, 'b_ada': b_ada, 'w_in': w_in, 'conv_w': conv_w,
            'gdn_conv_w': gdn_conv_w, 'gdn_a_log': gdn_a_log, 'gdn_dt_bias': gdn_dt_bias,
            'gdn_norm_w': gdn_norm_w, 'fox_f_bias': fox_f_bias, 'w_branch_a': w_branch_a,
            'w_branch_b': w_branch_b, 'w_branch_c': w_branch_c, 'w_o': w_o, 'ln1_g': ln1_g,
            'ln1_b': ln1_b, 'w_ff1': w_ff1, 'w_ff2': w_ff2, 'ln2_g': ln2_g, 'ln2_b': ln2_b}

def reference(x, c, w_ada, b_ada, w_in, conv_w, gdn_conv_w, gdn_a_log, gdn_dt_bias, gdn_norm_w,
              fox_f_bias, w_branch_a, w_branch_b, w_branch_c, w_o, ln1_g, ln1_b, w_ff1, w_ff2,
              ln2_g, ln2_b):
    split_points = np.cumsum(SPLIT_SIZES)[:-1].tolist()
    c_act = jax.nn.silu(c)
    for l in range(DEPTH):
        mod = c_act @ w_ada[l] + b_ada[l]
        shift1, scale1, gate1, shift2, scale2, gate2 = jnp.split(mod[:, None, :], 6, axis=-1)

        u = x * (1 + scale1) + shift1
        (cb, cc, ch, gq, gk, gv, gz, gb, ga, fq, fk, fv, ff, ma, mb, mc) = jnp.split(
            u @ w_in[l], split_points, axis=-1)
        y_a = short_conv_branch(cb, cc, ch, conv_w[l])
        y_b = gated_deltanet_branch(gq, gk, gv, gz, gb, ga, gdn_conv_w[l], gdn_a_log[l],
                                    gdn_dt_bias[l], gdn_norm_w[l])
        y_c = forgetting_attention_branch(fq, fk, fv, ff, fox_f_bias[l])
        merged = (jax.nn.sigmoid(ma) * (y_a @ w_branch_a[l])
                  + jax.nn.sigmoid(mb) * (y_b @ w_branch_b[l])
                  + jax.nn.sigmoid(mc) * (y_c @ w_branch_c[l]))
        x = layer_norm(DEEPNORM_ALPHA * x + gate1 * (merged @ w_o[l]), ln1_g[l], ln1_b[l])

        u = x * (1 + scale2) + shift2
        h = jnp.square(jax.nn.relu(u @ w_ff1[l]))
        x = layer_norm(DEEPNORM_ALPHA * x + gate2 * (h @ w_ff2[l]), ln2_g[l], ln2_b[l])
    return x


_drawn_inputs = setup_inputs


def setup_inputs(seed=0):
    import zlib

    import numpy as np

    out = dict(_drawn_inputs(seed))
    spreads = {}
    factors = {'b_ada': 3.296,
     'gdn_a_log': 8.0,
     'gdn_dt_bias': 5.622,
     'gdn_norm_w': 64.0,
     'fox_f_bias': 50.088,
     'ln1_g': 2.731,
     'ln1_b': 2.889,
     'ln2_g': 8.485,
     'ln2_b': 8.362,
     'w_branch_c': 2.789}
    for name, (base, spread) in spreads.items():
        noise = np.random.default_rng([zlib.crc32(name.encode()), seed]).standard_normal(out[name].shape)
        drawn = base * np.exp(spread * noise) if base else spread * noise
        out[name] = __import__('jax').numpy.asarray(drawn.astype(out[name].dtype))
    for name, factor in factors.items():
        out[name] = (out[name] * factor).astype(out[name].dtype)
    return out
```

```python
import concourse.bass as bass
from concourse import mybir
from contextlib import ExitStack
import math

F32 = mybir.dt.float32
F32R = mybir.dt.float32r
ALU = mybir.AluOpType
ACT = mybir.ActivationFunctionType

P = 128
S = 256
MT = S // P
D = 2048
KT = D // P
NC = 512
NCH = D // NC
BPC = NC // P
UK = 2
UPJ = KT // UK
RAWS = 4
PARTS = 4
LEAD = 3
DFF = 4 * D
VH = 32
DV = D // VH
CH = 64
NCK = S // CH
FH = 16
KPC = BPC
VPC = NC // DV
PAIRS = KPC // 2
LEVELS = 5
TAPS_A, TAPS_G = 3, 4
LN_EPS, NORM_EPS = 1e-5, 1e-6
LOG_TERMS = 8
ALPHA = 2.0 ** 0.25
BIG = 1e30
NMOD = 6 * NCH
NMOD_FIRST = 2 * NCH

OFF_CB, OFF_CC, OFF_CH = 0, D, 2 * D
OFF_GQ, OFF_GK, OFF_GV, OFF_GZ = 3 * D, 4 * D, 5 * D, 6 * D
OFF_BA = 7 * D
OFF_FQ = 7 * D + 2 * VH
OFF_FK, OFF_FV, OFF_F = OFF_FQ + D, OFF_FQ + 2 * D, OFF_FQ + 3 * D
OFF_MA = OFF_F + FH
NSM = 2 * VH + FH

MAIN_JOBS = (OFF_GQ, OFF_GK, OFF_GV, OFF_GZ, OFF_FQ, OFF_FK, OFF_FV, OFF_CC, OFF_CH, OFF_CB)
J_GQ, J_GK, J_GV, J_GZ, J_FQ, J_FK, J_FV, J_CC, J_CH, J_CB = range(10)
MAIN_UNITS = len(MAIN_JOBS) * UPJ
MODS = (NMOD - NMOD_FIRST) // NCH
MAIN_RAW = MAIN_UNITS + MODS * UPJ
MOD_START = 17
R_MAIN = NMOD_FIRST * UPJ
R_MERGE = R_MAIN + NCH * MAIN_RAW
R_OUT = R_MERGE + 3 * NCH * 2 * UPJ
R_FF = R_OUT + NCH * UPJ
J_MERGE = NCH * len(MAIN_JOBS)
J_OUT = J_MERGE + 3 * NCH * 2
J_FF = J_OUT + NCH
FFQ = DFF // D
FF_JOBS = 2 * NCH


def mod_after(u):
    return (u - MOD_START) // 2 if u >= MOD_START and (u - MOD_START) % 2 == 0 else None


def raw_place(u):
    return u + sum(mod_after(v) is not None for v in range(min(u, MAIN_UNITS)))


def plain_place(u):
    return u


class Signal:

    def __init__(self, sem, per):
        self.sem, self.per, self.made = sem, per, 0

    def value(self, i, k):
        return i * self.per + k


class Order:

    def __init__(self, eng, sem):
        self.eng, self.sem, self.base, self.i, self.pad, self.n, self.last = eng, sem, 0, 0, 0, 0, None

    def begin(self, i, pad):
        self.i, self.pad, self.n, self.last = i, pad, 0, None

    def do(self, ins, sig=None, k=None):
        if sig is None:
            self.n += 1
            ins.then_inc(self.sem, 1)
            self.last = (self.sem, self.i * self.pad + (self.base + self.n))
        else:
            sig.made += 1
            ins.then_inc(sig.sem, 1)
            self.last = (sig.sem, sig.value(self.i, k))

    def do_count(self, ins, sem, value):
        ins.then_inc(sem, 1)
        self.last = (sem, value)

    def after(self):
        if self.last is not None:
            self.eng.wait_ge(self.last[0], self.last[1])
            self.last = None

    def end(self, passes=1):
        assert 0 < self.n <= self.pad, (self.n, self.pad)
        self.after()
        self.eng.wait_ge(self.sem, self.i * self.pad + (self.base + self.n))
        if self.pad > self.n:
            self.eng.sem_inc(self.sem, self.pad - self.n)
        self.base += passes * self.pad
        self.i = 0


def layer_program(nc, x, c, w_ada, b_ada, w_in, conv_w, gdn_conv_w, gdn_a_log, gdn_dt_bias,
                  gdn_norm_w, fox_f_bias, w_branch_a, w_branch_b, w_branch_c, w_o, ln1_g, ln1_b,
                  w_ff1, w_ff2, ln2_g, ln2_b, out):
    ctx = ExitStack()
    with ctx:
        base = (nc.sbuf_base + 31) // 32 * 32
        top = [0]

        def sb(name, shape, dt=F32, at=None):
            size = (4 * math.prod(shape[1:]) + 31) // 32 * 32
            if at is None:
                at = top[0]
                top[0] += size
            assert base + at + size <= nc.sbuf_usable_end, (name, at, size, nc.sbuf_usable_end)
            return nc.alloc_sbuf_tensor_at(name, shape, dt, offset=base + at)

        def flat(t):
            return t[:, :, :].rearrange("p a b -> p (a b)")

        raw = sb("raw", [P, RAWS, UK, NC])
        w_hi = sb("w_hi", [P, PARTS, UK, NC], F32R)
        w_lo = sb("w_lo", [P, PARTS, UK, NC], F32R)
        u_hi = sb("u_hi", [P, KT, S], F32R)
        u_lo = sb("u_lo", [P, KT, S], F32R)
        y_at = top[0]
        yT = [sb(f"y_{b}_T", [P, KT, S]) for b in "abc"]
        ident = sb("ident", [P, P])
        ones = sb("ones", [P, P])
        upper = sb("upper", [P, P])
        chunk_upper = sb("chunk_upper", [P, P])
        level_mask = sb("level_mask", [P, LEVELS + 1, P])
        causal_big = sb("causal_big", [P, P])
        mod = sb("mod", [P, 6 * KT])
        bada = sb("bada", [P, 6 * KT])
        c_act = sb("c_act", [P, KT])
        cwg = sb("cwg", [P, TAPS_G, 3 * KT])
        cwa = sb("cwa", [P, TAPS_A, KT])
        norm_w = sb("norm_w", [P, DV])
        heads = sb("heads", [P, 5, MT, VH])
        cd = sb("cd", [P, NCK, VH])
        fcum = sb("fcum", [P, MT, FH])
        cur = sb("cur", [P, 5, MT, VPC])
        cur_cd = sb("cur_cd", [P, NCK, VPC])
        cur_f = sb("cur_f", [P, MT, KPC])
        cur_cwg = sb("cur_cwg", [P, 3, TAPS_G, BPC])
        cur_cwa = sb("cur_cwa", [P, TAPS_A, BPC])
        eps_b = sb("eps_b", [P, 4])
        fmax = sb("fmax", [P, 2, MT * KPC])
        rms = sb("rms", [P, MT * VPC])
        macc = sb("macc", [P, 2, NC])
        stage = sb("stage", [P, MT, NC])
        chunk_ones = sb("chunk_ones", [P, P], at=top[0] - 4 * MT * NC)
        half_rows = sb("half_rows", [P, 2, P], at=top[0] - 4 * MT * NC + 4 * P)
        tmp_at = top[0]
        QC = sb("QC", [P, BPC, S])
        KC = sb("KC", [P, BPC, S])
        VC = sb("VC", [P, BPC, S])
        FV = VC[:, :, :].rearrange("p (m b) s -> p m (b s)", m=MT)
        SZ = sb("SZ", [P, MT, NC])
        ktok = sb("ktok", [P, MT, NC])
        vtok = sb("vtok", [P, MT, NC])
        FQ = sb("FQ", [P, BPC, S])
        FK = sb("FK", [P, BPC, S])
        X = [dict() for _ in range(2)]
        for e in range(2):
            for n in ("V", "KB", "IT", "L", "B", "T", "TT"):
                X[e][n] = sb(f"{n}{e}", [P, 4, P])
            X[e]["VB"] = X[e]["L"][:, 0:2, :].rearrange("p a (b c) -> p (a b) c", c=DV)
            X[e]["UU"] = X[e]["T"][:, 0:2, :].rearrange("p a (b c) -> p (a b) c", c=DV)
            X[e]["VN"] = X[e]["T"][:, 2, :]
            X[e]["VS"] = X[e]["T"][:, 3, :]
            X[e]["WT"] = X[e]["B"]
            X[e]["ST"] = sb(f"ST{e}", [P, P])
            X[e]["O1"] = X[e]["V"][:, 0, :]
        at0 = top[0] - 4 * (2 * (7 * 4 * P + P))
        SC = sb("SC", [P, KPC, 3 * P], at=at0)
        BI = sb("BI", [P, KPC, 3 * P], at=at0 + 4 * KPC * 3 * P)
        PT = sb("PT", [P, KPC, 3 * P], at=at0 + 8 * KPC * 3 * P)
        osq = [X[1]["T"], X[1]["TT"]]
        norm_tmp = [flat(X[e][n]) for n in ("B", "T") for e in range(2)]
        slots_made = []
        x_sb = sb("x_sb", [P, MT, D], at=y_at)
        uT = sb("uT", [P, KT, S], at=y_at + 16384)
        ws = sb("ws", [P, KT, NSM], at=y_at + 32768)
        sm = sb("sm", [P, MT, NSM], at=y_at + 38000 // 32 * 32)
        sm2 = sb("sm2", [P, MT, NSM], at=y_at + 38688)
        rows = sb("rows", [P, 5, P], at=y_at + 39360)
        log_s = sb("log_s", [P, MT, NSM], at=tmp_at)
        log_s2 = sb("log_s2", [P, MT, NSM], at=tmp_at + 4 * MT * NSM)
        gpar = sb("gpar", [P, 2 * VH + FH], at=y_at + 41984)
        z_hi = sb("z_hi", [P, KT, S], F32R, at=tmp_at)
        z_lo = sb("z_lo", [P, KT, S], F32R, at=tmp_at + 16384)
        merged = sb("merged", [P, MT, D], at=tmp_at + 32768)
        sig = sb("sig", [P, MT, NC], at=tmp_at + 49152)
        gated = sb("gated", [P, MT, NC], at=tmp_at + 53248)
        x1 = sb("x1", [P, MT, D], at=y_at)
        xr = sb("xr", [P, MT, D], at=y_at + 16384)
        gate_b = sb("gate_b", [P, D], at=y_at + 32768)
        ln_g = sb("ln_g", [P, D], at=y_at + 40960)
        ln_b = sb("ln_b", [P, D], at=tmp_at + 49152)
        stats = sb("stats", [P, MT, NCH, 6], at=tmp_at + 57344)
        aggr = sb("aggr", [P, MT, 2], at=tmp_at + 57344 + 256)
        rstd = sb("rstd", [P, MT], at=tmp_at + 57344 + 288)
        turned2 = stage

        acc = [ctx.enter_context(nc.psum_tensor(f"acc{p}", [P, MT, NC], F32)) for p in range(2)]
        bank = [ctx.enter_context(nc.psum_tensor(f"bank{p}", [P, NC], F32)) for p in range(4)]

        def signal(name, per=1):
            return Signal(ctx.enter_context(nc.semaphore(name)), per)

        raw_ready = [signal(f"raw_ready{s}") for s in range(RAWS)]
        raw_free, hi_ready, lo_ready, units_used = (
            signal(n) for n in ("raw_free", "hi_ready", "lo_ready", "units_used"))
        acc_free = [signal(f"acc_free{p}") for p in range(2)]
        own = {n: ctx.enter_context(nc.semaphore(f"{n}_order")) for n in ("act", "dve", "pool")}
        met = {n: signal(f"{n}_met") for n in ("pe", "act", "dve", "pool")}
        x_in, p_in, ws_in, ln_in, stored, slots_granted = (
            signal(n) for n in ("x_in", "p_in", "ws_in", "ln_in", "stored", "slots_granted"))
        N = {}
        for name, per in dict(
                rows_turned=1, rows_in=1, macc_first=1, mcol_first=1, mod_first=1, x_turned=1, u_made=1,
                u_hi_made=1, u_lo_made=1, small_done=1, small_in=1, small_neg=1, small_exp=1, small_sp=1, logs_made=1,
                sums_done=1, sums_in=1, decay_left=1, ln_var=1, ln_rstd=1, ln_ready=1,
                macc_ready=MODS, mcol_done=MODS, mod_made=MODS,
                turned=3, conv_made=3, silu_made=3, sq_made=1, ssq_done=1, rn_made=1, qk_made=1,
                tok_done=2, k_tok_in=1, v_tok_in=1,
                kk_done=4, gb_done=4, d_made=4, decay_made=4, low_made=4, it_made=4, it_masked=4,
                low_turned=4, l_made=4, b_made=4 * (LEVELS + 1), t1_made=4, t1_turned=4, tt1_made=4,
                v_done=4 * LEVELS, v_made=4 * LEVELS, dtt_done=4 * LEVELS, dt_done=4 * LEVELS,
                tt_made=4 * LEVELS, t_made=4 * LEVELS, kb_made=4, vb_made=4,
                wt_done=4, wt_made=4, u_done=4, uu_made=4,
                ws_done=4 * NCK, qs_done=4 * NCK, vs_made=4 * NCK, o1_made=4 * NCK,
                in_done=4 * NCK, su_done=4 * NCK, s_made=4 * NCK, s_zero=4, o_made=4 * NCK,
                osq_made=MT, rms_in=1, rms_out=1, rms_used=1, yb_tok=MT, yb_turned=1, yb_made=1,
                f_turned=2, f_made=2, fv_made=1, cum_done=1, bias_made=1, scores_done=1, fmax_made=1,
                fexp_made=1, prob_made=1, prob_turned=1, probT_made=1, yc_done=1, yc_made=1,
                c_turned=3, cc_made=1, ch_made=1, conv3_made=1, ya_made=1,
                y_hi=1, y_lo=1, z_turned=1, z_hi_made=1, z_lo_made=1, gate_done=1, gate_made=1,
                x1_turned=1, x1_scaled=1, u2_hi=1, u2_lo=1, squared=NCH, h_turned=NCH, h_hi=NCH,
                h_lo=UPJ).items():
            N[name] = signal(name, per)
        fences = {n: signal(f"{n}_fence", 6) for n in ("pe", "act", "dve", "pool")}

        block = ctx.enter_context(nc.Block())

        w_in_t = w_in[0].rearrange("(k p) n -> p k n", p=P)
        w_ada_t = w_ada[0].rearrange("(k p) n -> p k n", p=P)
        w_br_t = [w[0].rearrange("(k p) n -> p k n", p=P) for w in (w_branch_a, w_branch_b, w_branch_c)]
        w_o_t = w_o[0].rearrange("(k p) n -> p k n", p=P)
        w_ff1_t = w_ff1[0].rearrange("(k p) n -> p k n", p=P)
        w_ff2_t = w_ff2[0].rearrange("(k p) n -> p k n", p=P)

        def meet(eng, me, n, order=None):
            if order is not None:
                order.after()
            eng.sem_inc(met[me].sem, 1)
            for other in met:
                if other != me:
                    eng.wait_ge(met[other].sem, n)

        def fence(eng, me, i, n, order=None):
            if order is not None:
                order.after()
            eng.sem_inc(fences[me].sem, 1)
            for other in fences:
                if other != me:
                    eng.wait_ge(fences[other].sem, fences[other].value(i, n))

        def bank4(b):
            return bank[b][:, :].rearrange("p (a b) -> p a b", a=4)

        def job_wait(eng, j):
            eng.wait_ge(units_used.sem, j * UPJ + (PARTS + UPJ))

        @block.sync
        def _(sp):
            sp.dma_start(rows[0:6 * KT, 0, :], b_ada[0].rearrange("(r p) -> r p", p=P)).then_inc(p_in.sem, 16)
            taps = gdn_conv_w[0].rearrange("w (r p) -> (w r) p", p=P)
            for h in range(2):
                sp.dma_start(rows[0:96, 1 + h, :], taps[96 * h:96 * h + 96, :]).then_inc(p_in.sem, 16)
            sp.dma_start(rows[0:TAPS_A * KT, 3, :], conv_w[0].rearrange("w (r p) -> (w r) p", p=P)).then_inc(p_in.sem, 16)
            sp.dma_start(rows[0:KT, 4, :], c[0].rearrange("(r p) -> r p", p=P)).then_inc(p_in.sem, 16)
            for at, n, src in ((0, VH, gdn_a_log), (VH, VH, gdn_dt_bias), (2 * VH, FH, fox_f_bias)):
                sp.dma_start(gpar[:, at:at + n], src[0].partition_broadcast(P)).then_inc(p_in.sem, 16)
            sp.dma_start(norm_w[:, :], gdn_norm_w[0].partition_broadcast(P)).then_inc(p_in.sem, 16)

            def load(r, rl, src, k0, col):
                if not isinstance(col, int):
                    col = sp.snap(col)
                if not isinstance(k0, int):
                    k0 = sp.snap(k0)
                sp.wait_ge(raw_free.sem, r + 1)
                sp.sem_inc(slots_granted.sem, 1)
                sp.dma_start(raw[:, rl % RAWS, :, :], src[:, bass.ds(k0, UK), bass.ds(col, NC)]
                             ).then_inc(raw_ready[rl % RAWS].sem, 16)

            with sp.Fori(0, NMOD_FIRST) as i:
                for u in range(UPJ):
                    load(i * UPJ + u, u, w_ada_t, UK * u, i * NC)
            sp.dma_start(x_sb[:, :, :], x[0].rearrange("(m p) n -> p m n", p=P)).then_inc(x_in.sem, 16)
            sp.dma_start(ws[:, :, 0:2 * VH], w_in_t[:, :, OFF_BA:OFF_BA + 2 * VH]).then_inc(ws_in.sem, 16)
            sp.dma_start(ws[:, :, 2 * VH:NSM], w_in_t[:, :, OFF_F:OFF_F + FH]).then_inc(ws_in.sem, 16)
            with sp.Fori(0, NCH) as i:
                r = 0
                for u in range(MAIN_UNITS):
                    load(i * MAIN_RAW + (R_MAIN + r), r, w_in_t, UK * (u % UPJ), i * NC + MAIN_JOBS[u // UPJ])
                    r += 1
                    m = mod_after(u)
                    if m is not None:
                        load(i * MAIN_RAW + (R_MAIN + r), r, w_ada_t, UK * (m % UPJ),
                             i * (MODS * NC) + (NMOD_FIRST + m // UPJ) * NC)
                        r += 1
            for b in range(3):
                with sp.Fori(0, NCH) as i:
                    for u in range(2 * UPJ):
                        src, col = (w_in_t, i * NC + (OFF_MA + b * D)) if u < UPJ else (w_br_t[b], i * NC)
                        load(i * (2 * UPJ) + (R_MERGE + b * NCH * 2 * UPJ + u), u, src, UK * (u % UPJ), col)
            with sp.Fori(0, NCH // 2) as i:
                for u in range(2 * UPJ):
                    load(i * (2 * UPJ) + (R_OUT + u), u, w_o_t, UK * (u % UPJ), i * (2 * NC) + u // UPJ * NC)
            with sp.Fori(0, FFQ) as q:
                for j in range(FF_JOBS):
                    for u in range(UPJ):
                        r = q * (FF_JOBS * UPJ) + (R_FF + j * UPJ + u)
                        if j < NCH:
                            load(r, u, w_ff1_t, UK * u, q * D + j * NC)
                        else:
                            load(r, u, w_ff2_t, q * KT + UK * u, (j - NCH) * NC)
            for u in range(LEAD):
                load(R_FF + FFQ * FF_JOBS * UPJ + u, u, w_ff1_t, UK * u, 0)
            for m in range(MT):
                sp.wait_ge(N["ln_ready"].sem, MT + m + 1)
                sp.dma_start(out[0, m * P:(m + 1) * P, :], x1[:, m, :]).then_inc(stored.sem, 16)
            sp.wait_ge(stored.sem, 16 * MT)

        @block.gpsimd
        def _(pool):
            o = Order(pool, own["pool"])
            g = nc.gpsimd
            o.begin(0, 60)
            for t, v in ((ident, 0.0), (ones, 1.0), (upper, 1.0), (chunk_upper, 1.0), (chunk_ones, 1.0)):
                o.do(g.memset(t[:, :], v))
            o.do(g.memset(half_rows[:, :, :], 1.0))
            o.do(g.memset(level_mask[:, :, :], 0.0))
            o.do(g.memset(causal_big[:, :], 0.0))
            for n, v in enumerate((NORM_EPS, -0.5 * math.log(P), LN_EPS, 1.0)):
                o.do(g.memset(eps_b[:, n:n + 1], v))
            o.after()

            def keep(t, pattern, start, cm, fill=0.0, op=ALU.is_ge):
                o.do(g.affine_select(out=t, in_=t, compare_op=op, fill=fill, base=start, pattern=pattern,
                                     channel_multiplier=cm))
                o.after()

            keep(ident[:, :], [[-1, P]], 0, 1, 1.0, ALU.not_equal)
            keep(upper[:, :], [[1, P]], 0, -1)
            for t in (chunk_upper, chunk_ones):
                v = t[:, :].rearrange("p (b c) -> p b c", c=CH)
                keep(v, [[-CH, 2], [0, CH]], 0, 1)
                keep(v, [[CH, 2], [0, CH]], CH - 1, -1)
            keep(chunk_upper[:, :], [[1, P]], 0, -1)
            keep(half_rows[:, 0, :], [[0, P]], CH - 1, -1)
            keep(half_rows[:, 1, :], [[0, P]], -CH, 1)
            keep(causal_big[:, :], [[-1, P]], 0, 1, BIG)
            for l in range(LEVELS + 1):
                s = 1 << l
                v = level_mask[:, l, :].rearrange("p (b h c) -> p b h c", h=2, c=s)[:, :, 0, :]
                o.do(g.memset(v, 1.0))
                o.after()
                keep(v, [[-2 * s, P // (2 * s)], [0, s]], -s, 1)
                keep(v, [[2 * s, P // (2 * s)], [0, s]], 2 * s - 1, -1)
            o.end()
            meet(pool, "pool", 1, o)
            meet(pool, "pool", 2, o)
            meet(pool, "pool", 3, o)

            with pool.Fori(0, NCH) as i:
                o.begin(i, 40)

                def wait(name, k):
                    pool.wait_ge(N[name].sem, N[name].value(i, k))

                fence(pool, "pool", i, 1, o)
                fence(pool, "pool", i, 2, o)
                for pair in range(PAIRS):
                    fence(pool, "pool", i, 3 + pair, o)
                    for e in range(2):
                        k = 2 * pair + e
                        xe = X[e]

                        def scale_by(n, width):
                            return cur[:, n, :, 2 * k:2 * k + 2].unsqueeze(3).broadcast_to([P, MT, 2, width])

                        wait("l_made", k + 1)
                        mask = [level_mask[:, l, :].unsqueeze(1).broadcast_to([P, 4, P]) for l in range(LEVELS + 1)]
                        o.do(g.tensor_tensor(xe["B"][:, :, :], xe["L"][:, :, :], mask[0], ALU.mult),
                             N["b_made"], pair * 12 + e + 1)
                        o.do(g.memset(xe["ST"][:, :], 0.0), N["s_zero"], k + 1)
                    for e in range(2):
                        k = 2 * pair + e
                        xe = X[e]
                        wait("it_made", k + 1)
                        o.do(g.tensor_tensor(xe["IT"][:, :, :], xe["IT"][:, :, :],
                                             chunk_upper[:, :].unsqueeze(1).broadcast_to([P, 4, P]), ALU.mult),
                             N["it_masked"], k + 1)
                    for l in range(LEVELS):
                        for e in range(2):
                            k = 2 * pair + e
                            xe = X[e]
                            if l == 0:
                                wait("t1_made", k + 1)
                            else:
                                wait("v_done", pair * 2 * LEVELS + 2 * (l - 1) + e + 1)
                            o.do(g.tensor_tensor(xe["B"][:, :, :], xe["L"][:, :, :], mask[l + 1], ALU.mult),
                                 N["b_made"], pair * 12 + 2 * (l + 1) + e + 1)
                            if l == 1:
                                kk = ktok[:, :, k * P:(k + 1) * P].unsqueeze(2).broadcast_to([P, MT, 2, P])
                                o.do(g.tensor_tensor(xe["KB"][:, :, :].rearrange("p (t r) c -> p t r c", r=2), kk,
                                                     cur[:, 3, :, 2 * k:2 * k + 2].unsqueeze(3).broadcast_to([P, MT, 2, P]),
                                                     ALU.mult), N["kb_made"], k + 1)
                    for e in range(2):
                        k = 2 * pair + e
                        xe = X[e]
                        pool.wait_ge(N["b_made"].sem, N["b_made"].value(i, pair * 12 + 12))
                        vv = vtok[:, :, k * P:(k + 1) * P].rearrange("p t (r c) -> p t r c", r=2)
                        o.do(g.tensor_tensor(xe["VB"].rearrange("p (t r) c -> p t r c", r=2), vv,
                                             cur[:, 2, :, 2 * k:2 * k + 2].unsqueeze(3).broadcast_to([P, MT, 2, DV]),
                                             ALU.mult), N["vb_made"], k + 1)
                fence(pool, "pool", i, 5, o)
                for m in range(MT):
                    o.do(g.tensor_tensor(flat(osq[m]), vtok[:, m, :], vtok[:, m, :], ALU.mult), N["osq_made"], m + 1)
                nw = norm_w[:, :].unsqueeze(1).broadcast_to([P, VPC, DV])
                for m in range(MT):
                    z = SZ[:, m, :].rearrange("p (h d) -> p h d", d=DV)
                    o.do(g.tensor_tensor(z, z, nw, ALU.mult))
                o.after()
                wait("rms_used", 1)
                for m in range(MT):
                    o.do(g.tensor_tensor(vtok[:, m, :], vtok[:, m, :], SZ[:, m, :], ALU.mult), N["yb_tok"], m + 1)
                fence(pool, "pool", i, 6, o)
                o.end(NCH)
            meet(pool, "pool", 4, o)
            meet(pool, "pool", 5, o)
            meet(pool, "pool", 6, o)
            meet(pool, "pool", 7, o)

        @block.scalar
        def _(act):
            o = Order(act, own["act"])
            a = nc.scalar

            def activate(dst, src, func, name=None, k=None, **kw):
                o.do(a.activation(dst, src, func, **kw), N[name] if name else None, k)

            def hi_unit(n, u, r, rl):
                act.wait_ge(raw_ready[rl % RAWS].sem, r)
                act.wait_ge(units_used.sem, n + 1)
                a.activation(w_hi[:, u % PARTS, :, :], raw[:, rl % RAWS, :, :], ACT.Copy).then_inc(hi_ready.sem, 1)

            def slots(i, units, unit0, raws, raw0, place, count):
                def go_on():
                    s = count[0]
                    count[0] += 1
                    if s % 2 and s // 2 < units:
                        u = s // 2 + LEAD
                        rl = place(u)
                        hi_unit(i * units + (unit0 + u), u, i * (16 * raws // RAWS) + 16 * ((raw0 + rl) // RAWS + 1), rl)
                return go_on

            o.begin(0, 60)
            act.wait_ge(N["rows_turned"].sem, 1)
            activate(bada[:, :], bank[0][:, 0:96], ACT.Copy)
            activate(flat(cwg), bank[0][:, 96:288], ACT.Copy)
            activate(flat(cwa), bank[0][:, 288:336], ACT.Copy)
            activate(c_act[:, :], bank[0][:, 336:336 + KT], ACT.Silu, "rows_in", 1)
            o.end()
            meet(act, "act", 1, o)
            o.begin(0, 60)
            act.wait_ge(N["mod_first"].sem, NMOD_FIRST + 1)
            for k in range(KT):
                if k % 2 == 0:
                    act.wait_ge(N["x_turned"].sem, k // 2 + 1)
                activate(uT[:, k, :], bank[k // 2 % 4][:, (k % 2) * S:(k % 2 + 1) * S], ACT.Identity,
                         "u_made", k + 1, scale=mod[:, KT + k:KT + k + 1], bias=mod[:, k:k + 1])
            o.after()
            for k in range(4):
                activate(u_hi[:, 4 * k:4 * k + 4, :], uT[:, 4 * k:4 * k + 4, :], ACT.Copy, "u_hi_made", k + 1)
            meet(act, "act", 2, o)
            act.wait_ge(N["small_done"].sem, 1)
            activate(flat(sm), bank[0][:, 0:MT * NSM], ACT.Copy, "small_in", 1)
            activate(gpar[:, 0:VH], gpar[:, 0:VH], ACT.Exp)
            act.wait_ge(N["small_neg"].sem, 1)
            activate(flat(sm), flat(sm), ACT.Exp, "small_exp", 1)
            act.wait_ge(N["small_sp"].sem, 1)
            activate(heads[:, 2, :, :], sm2[:, :, 0:VH], ACT.Exp, scale=-1.0)
            act.wait_ge(N["sums_done"].sem, 1)
            decay_sums = bank[1][:, 0:MT * VH].rearrange("p (m h) -> p m h", m=MT)
            activate(heads[:, 0, :, :], decay_sums, ACT.Copy)
            activate(heads[:, 1, :, :], decay_sums, ACT.Exp)
            activate(flat(cd), bank[2][:, 0:NCK * VH], ACT.Exp)
            activate(flat(fcum), bank[3][:, 0:MT * FH], ACT.Copy, "sums_in", 1)
            act.wait_ge(N["decay_left"].sem, 1)
            activate(heads[:, 4, :, :], heads[:, 4, :, :], ACT.Exp)
            o.end()
            meet(act, "act", 3, o)

            for u in range(LEAD):
                hi_unit(u, u, 16 * ((R_MAIN + u) // RAWS + 1), u)

            with act.Fori(0, NCH) as i:
                o.begin(i, 90)
                count = [0]
                next_slot = slots(i, MAIN_UNITS, 0, MAIN_RAW, R_MAIN, raw_place, count)

                def wait(name, k):
                    act.wait_ge(N[name].sem, N[name].value(i, k))

                def until(job):
                    while count[0] < (job + 1) * KT:
                        next_slot()

                def take_job(job, dst, func=ACT.Copy):
                    until(job)
                    job_wait(act, i * len(MAIN_JOBS) + job)
                    o.do_count(a.activation(dst, acc[job % 2][:, :, :], func),
                               acc_free[job % 2].sem, i * (len(MAIN_JOBS) // 2) + (job // 2 + 2))

                fence(act, "act", i, 1, o)
                for k, job in enumerate((J_GQ, J_GK, J_GV)):
                    if k:
                        wait("turned", k)
                    take_job(job, stage[:, :, :])
                    next_slot()
                    next_slot()
                    next_slot()
                    dst = (QC, KC, VC)[k]
                    wait("conv_made", k + 1)
                    activate(dst[:, :, :], dst[:, :, :], ACT.Silu, "silu_made", k + 1)
                take_job(J_GZ, SZ[:, :, :], ACT.Silu)
                for n in range(4):
                    src = (QC, KC)[n // 2][:, 2 * (n % 2):2 * (n % 2) + 2, :]
                    activate(norm_tmp[n], src.rearrange("p a b -> p (a b)"), ACT.Square, *(("sq_made", 1) if n == 3 else ()))
                next_slot()
                next_slot()
                wait("ssq_done", 1)
                for n in range(4):
                    activate(norm_tmp[n], bank[n][:, :], ACT.Ln, bias=eps_b[:, 0:1])
                next_slot()
                o.after()
                for n in range(4):
                    kw = dict(bias=eps_b[:, 1:2]) if n < 2 else {}
                    activate(norm_tmp[n], norm_tmp[n], ACT.Exp, *(("rn_made", 1) if n == 3 else ()), scale=-0.5, **kw)
                next_slot()
                next_slot()
                wait("tok_done", 1)
                for m in range(MT):
                    activate(ktok[:, m, :], bank[m][:, :], ACT.Copy, *(("k_tok_in", 1) if m else ()))
                next_slot()
                fence(act, "act", i, 2, o)
                next_slot()

                def delta_pair(pair):
                    fence(act, "act", i, 3 + pair, o)
                    next_slot()
                    for e in range(2):
                        k = 2 * pair + e
                        wait("d_made", k + 1)
                        activate(X[e]["V"][:, :, :], X[e]["V"][:, :, :], ACT.Exp, "decay_made", k + 1)
                    next_slot()
                    for e in range(2):
                        k = 2 * pair + e
                        wait("low_turned", k + 1)
                        for q in range(4):
                            t, r = divmod(q, 2)
                            activate(X[e]["L"][:, q, :], bank[e][:, q * P:(q + 1) * P], ACT.Copy,
                                     *(("l_made", k + 1) if q == 3 else ()),
                                     scale=cur[:, 2, t, 2 * k + r:2 * k + r + 1])
                    next_slot()
                    next_slot()
                    for e in range(2):
                        k = 2 * pair + e
                        wait("t1_turned", k + 1)
                        activate(flat(X[e]["TT"]), bank[2 + e][:, :], ACT.Copy, "tt1_made", k + 1)
                    next_slot()
                    for l in range(LEVELS):
                        for e in range(2):
                            n = pair * 2 * LEVELS + 2 * l + e + 1
                            wait("v_done", n)
                            activate(flat(X[e]["V"]), bank[e][:, :], ACT.Copy, "v_made", n)
                        next_slot()
                        next_slot()
                    for e in range(2):
                        k = 2 * pair + e
                        wait("wt_done", k + 1)
                        activate(flat(X[e]["WT"]), bank[e][:, :], ACT.Copy, "wt_made", k + 1)
                    next_slot()
                    for j in range(NCK):
                        t, h = divmod(j, 2)
                        rows_ = slice(CH * h, CH * h + CH)
                        for e in range(2):
                            k = 2 * pair + e
                            n = pair * 2 * NCK + 2 * j + e + 1
                            wait("qs_done", n)
                            if j:
                                wait("o_made", n - 2)
                            for r in range(2):
                                activate(X[e]["O1"][rows_, r * DV:(r + 1) * DV],
                                         bank[2 + e][rows_, P + r * DV:P + (r + 1) * DV],
                                         ACT.Copy, *(("o1_made", n) if r else ()),
                                         scale=cur[rows_, 1, t, 2 * k + r:2 * k + r + 1])
                        next_slot()
                        next_slot()

                delta_pair(0)
                for n, job in enumerate((J_FQ, J_FK)):
                    if n:
                        wait("f_turned", n)
                    take_job(job, stage[:, :, :])
                    next_slot()
                    next_slot()
                delta_pair(1)
                fence(act, "act", i, 5, o)
                take_job(J_FV, FV)
                wait("rms_in", 1)
                activate(rms[:, :], rms[:, :], ACT.Ln, bias=eps_b[:, 0:1], scale=1.0 / DV)
                o.after()
                activate(rms[:, :], rms[:, :], ACT.Exp, "rms_out", 1, scale=-0.5)
                next_slot()
                next_slot()
                next_slot()
                wait("yb_turned", 1)
                for h in range(2):
                    activate(yT[1][:, bass.ds(i * BPC + 2 * h, 2), :],
                             bank[h][:, :].rearrange("p (a b) -> p a b", a=2), ACT.Copy,
                             *(("yb_made", 1) if h else ()))
                next_slot()
                next_slot()
                wait("fmax_made", 1)
                for f in range(KPC):
                    for t in range(MT):
                        s_ = SC[:, f, t * P:(1 + 2 * t) * P]
                        activate(s_, s_, ACT.Exp, bias=fmax[:, 0, MT * f + t:MT * f + t + 1],
                                 accum_out=fmax[:, 1, MT * f + t:MT * f + t + 1])
                o.after()
                act.sem_inc(N["fexp_made"].sem, 1)
                next_slot()
                wait("prob_turned", 1)
                for f in range(KPC):
                    activate(PT[:, f, :], bank[f][:, 0:3 * P], ACT.Copy, *(("probT_made", 1) if f == KPC - 1 else ()))
                next_slot()
                next_slot()
                fence(act, "act", i, 6, o)
                for n, job in enumerate((J_CC, J_CH, J_CB)):
                    if n:
                        wait("c_turned", n)
                    take_job(job, stage[:, :, :])
                    next_slot()
                    next_slot()
                assert count[0] >= 2 * MAIN_UNITS
                slots_made.append(count[0])
                o.end(NCH)
            meet(act, "act", 4, o)

            def hi_split(dst, src, name, first):
                for n in range(4):
                    activate(dst[:, 4 * n:4 * n + 4, :], src[:, 4 * n:4 * n + 4, :], ACT.Copy, name, first + n)

            for b in range(3):
                o.begin(0, 10)
                if b:
                    job_wait(act, J_MERGE + 2 * NCH * b - 1)
                hi_split(z_hi, yT[b], "y_hi", 4 * b + 1)
                o.do(a.activation(rms[:, 0:1], eps_b[:, 0:1], ACT.Copy))
                o.end()
                with act.Fori(0, NCH) as i:
                    o.begin(i, 10)
                    count = [0]
                    next_slot = slots(i, 2 * UPJ, J_MERGE * UPJ + b * 2 * UPJ * NCH, 2 * UPJ,
                                      R_MERGE + b * 2 * UPJ * NCH, plain_place, count)
                    for _ in range(KT + 1):
                        next_slot()
                    j = J_MERGE + 2 * NCH * b
                    job_wait(act, i * 2 + j)
                    act.wait_ge(acc_free[1].sem, i + (j // 2 + 1))
                    o.do_count(a.activation(sig[:, :, :], acc[0][:, :, :], ACT.Sigmoid),
                               acc_free[0].sem, i + (j // 2 + 2))
                    while count[0] < 4 * UPJ:
                        next_slot()
                    o.do(a.activation(rms[:, 0:1], eps_b[:, 0:1], ACT.Copy))
                    o.end(NCH)
            meet(act, "act", 5, o)
            act.dma_start(x1[:, :, :], x[0].rearrange("(m p) n -> p m n", p=P)).then_inc(ln_in.sem, 16)
            act.dma_start(ln_g[:, :], ln1_g[0].partition_broadcast(P)).then_inc(ln_in.sem, 16)
            act.dma_start(ln_b[:, :], ln1_b[0].partition_broadcast(P)).then_inc(ln_in.sem, 16)
            o.begin(0, 40)
            for n in range(8):
                act.wait_ge(N["z_turned"].sem, n + 1)
                activate(z_hi[:, 2 * n:2 * n + 2, :], bank[n % 4][:, :].rearrange("p (a b) -> p a b", a=2), ACT.Copy, "z_hi_made", n + 1)

            def gate_rows(which):
                for n in range(NCH):
                    act.wait_ge(N["gate_done"].sem, which * NCH + n + 1)
                    activate(gate_b[:, n * NC:(n + 1) * NC], bank[n][:, :], ACT.Copy, "gate_made", which * NCH + n + 1)

            gate_rows(0)
            activate(rms[:, 0:1], eps_b[:, 0:1], ACT.Copy)
            o.end()
            with act.Fori(0, NCH // 2) as i:
                count = [0]
                next_slot = slots(i, 2 * UPJ, J_OUT * UPJ, 2 * UPJ, R_OUT, plain_place, count)
                while count[0] < 4 * UPJ:
                    next_slot()

            def ln_scale(which):
                for m in range(MT):
                    act.wait_ge(N["ln_var"].sem, which * MT + m + 1)
                    activate(rstd[:, m:m + 1], aggr[:, m, 1:2], ACT.Ln, bias=eps_b[:, 2:3])
                    o.after()
                    activate(rstd[:, m:m + 1], rstd[:, m:m + 1], ACT.Exp, "ln_rstd", which * MT + m + 1, scale=-0.5)

            o.begin(0, 60)
            ln_scale(0)
            for n in range(8):
                act.wait_ge(N["x1_turned"].sem, n + 1)
                if n >= 2:
                    act.wait_ge(N["u2_lo"].sem, n - 1)
                for q in range(2):
                    k = 2 * n + q
                    activate(gated[:, n % 2, q * S:(q + 1) * S], bank[n % 4][:, q * S:(q + 1) * S], ACT.Identity,
                             *(("x1_scaled", n + 1) if q else ()),
                             scale=mod[:, 4 * KT + k:4 * KT + k + 1], bias=mod[:, 3 * KT + k:3 * KT + k + 1])
                o.after()
                activate(u_hi[:, 2 * n:2 * n + 2, :], gated[:, n % 2, :].rearrange("p (a b) -> p a b", a=2), ACT.Copy, "u2_hi", n + 1)
            gate_rows(1)
            o.do(a.activation(rms[:, 0:1], eps_b[:, 0:1], ACT.Copy))
            o.end()
            meet(act, "act", 6, o)
            act.dma_start(ln_g[:, :], ln2_g[0].partition_broadcast(P)).then_inc(ln_in.sem, 16)
            act.dma_start(ln_b[:, :], ln2_b[0].partition_broadcast(P)).then_inc(ln_in.sem, 16)
            with act.Fori(0, FFQ) as i:
                o.begin(i, 60)
                count = [0]
                next_slot = slots(i, FF_JOBS * UPJ, J_FF * UPJ, FF_JOBS * UPJ, R_FF, plain_place, count)
                for j in range(NCH):
                    while count[0] < (j + 1) * KT:
                        next_slot()
                    job_wait(act, i * FF_JOBS + (J_FF + j))
                    if j:
                        act.wait_ge(N["h_turned"].sem, N["h_turned"].value(i, j))
                    o.do_count(a.activation(stage[:, :, :], acc[j % 2][:, :, :], ACT.Relu),
                               acc_free[j % 2].sem, i * (FF_JOBS // 2) + ((J_FF + j) // 2 + 2))
                    o.after()
                    activate(stage[:, :, :], stage[:, :, :], ACT.Square, "squared", j + 1)
                    next_slot()
                    next_slot()
                    act.wait_ge(N["h_turned"].sem, N["h_turned"].value(i, j + 1))
                    for h in range(2):
                        activate(z_hi[:, 4 * j + 2 * h:4 * j + 2 * h + 2, :],
                                 bank[2 * (j % 2) + h][:, :].rearrange("p (a b) -> p a b", a=2), ACT.Copy,
                                 *(("h_hi", j + 1) if h else ()))
                while count[0] < FF_JOBS * KT:
                    next_slot()
                o.end(FFQ)
            meet(act, "act", 7, o)
            o.begin(0, 20)
            ln_scale(1)
            o.do(a.activation(rms[:, 0:1], eps_b[:, 0:1], ACT.Copy))
            o.end()

        @block.vector
        def _(dve):
            o = Order(dve, own["dve"])
            v = nc.vector

            def tt(dst, in0, in1, op, name=None, k=None):
                o.do(v.tensor_tensor(dst, in0, in1, op), N[name] if name else None, k)

            def ts(dst, in0, s1, s2, op0, op1=ALU.bypass, name=None, k=None):
                o.do(v.tensor_scalar(dst, in0, s1, s2, op0, op1), N[name] if name else None, k)

            def stt(dst, in0, scalar, in1, op0, op1, name=None, k=None):
                o.do(v.scalar_tensor_tensor(dst, in0, scalar, in1, op0, op1), N[name] if name else None, k)

            def copy(dst, src, name=None, k=None):
                o.do(v.tensor_copy(dst, src), N[name] if name else None, k)

            def lo_unit(n, u, rl):
                dve.wait_ge(hi_ready.sem, n + 1)
                dve.wait_ge(units_used.sem, n + 1)
                v.tensor_tensor(w_lo[:, u % PARTS, :, :], raw[:, rl % RAWS, :, :], w_hi[:, u % PARTS, :, :],
                                ALU.subtract).then_inc(lo_ready.sem, 1)
                dve.wait_ge(lo_ready.sem, n + 1)
                dve.sem_inc(raw_free.sem, 1)

            def mod_unit(m, r, rl, into):
                dve.wait_ge(raw_ready[rl % RAWS].sem, r)
                for q in range(UK):
                    k = UK * m + q
                    src = raw[:, rl % RAWS, q, :]
                    o.after()
                    if k == 0:
                        ts(into, src, c_act[:, 0:1], None, ALU.mult)
                    else:
                        stt(into, src, c_act[:, k:k + 1], into, ALU.mult, ALU.add)
                o.after()
                dve.sem_inc(raw_free.sem, 1)

            def slots(i, units, unit0, raws, raw0, place, count):
                def go_on():
                    s = count[0]
                    count[0] += 1
                    if s % 2 and s // 2 < units:
                        u = s // 2 + LEAD
                        rl = place(u)
                        lo_unit(i * units + (unit0 + u), u, rl)
                        m = mod_after(u) if place is raw_place and u < MAIN_UNITS else None
                        if m is not None:
                            n = m // UPJ
                            if m % UPJ == 0 and n >= 2:
                                dve.wait_ge(N["mcol_done"].sem, N["mcol_done"].value(i, n - 1))
                            rl += 1
                            mod_unit(m % UPJ, i * (16 * raws // RAWS) + 16 * ((raw0 + rl) // RAWS + 1), rl, macc[:, n % 2, :])
                            if m % UPJ == UPJ - 1:
                                dve.sem_inc(N["macc_ready"].sem, 1)
                return go_on

            dve.sem_inc(raw_free.sem, RAWS)
            meet(dve, "dve", 1, o)
            with dve.Fori(0, NMOD_FIRST) as i:
                o.begin(i, 20)
                dve.wait_ge(N["rows_in"].sem, 1)
                for m in range(UPJ):
                    mod_unit(m, i * (16 * UPJ // RAWS) + 16 * (m // RAWS + 1), m, macc[:, 0, :])
                dve.sem_inc(N["macc_first"].sem, 1)
                dve.wait_ge(N["mcol_first"].sem, i + 1)
                tt(mod[:, bass.ds(i * BPC, BPC)], bank[0][:, 0:BPC], bada[:, bass.ds(i * BPC, BPC)], ALU.add)
                o.end(NMOD_FIRST)
                dve.sem_inc(N["mod_first"].sem, 1)
            o.begin(0, 40)
            ts(mod[:, KT:2 * KT], mod[:, KT:2 * KT], 1.0, None, ALU.add, name="mod_first", k=NMOD_FIRST + 1)
            for k in range(4):
                dve.wait_ge(N["u_hi_made"].sem, k + 1)
                tt(u_lo[:, 4 * k:4 * k + 4, :], uT[:, 4 * k:4 * k + 4, :], u_hi[:, 4 * k:4 * k + 4, :], ALU.subtract, "u_lo_made", k + 1)
            meet(dve, "dve", 2, o)
            dve.wait_ge(N["small_in"].sem, 1)

            def both(t):
                return t.unsqueeze(1).broadcast_to([P, MT, t.shape[1]])

            ts(sm2[:, :, 0:VH], sm[:, :, 0:VH], -1.0, None, ALU.mult)
            tt(sm2[:, :, VH:2 * VH], sm[:, :, VH:2 * VH], both(gpar[:, VH:2 * VH]), ALU.add)
            stt(sm2[:, :, 2 * VH:NSM], sm[:, :, 2 * VH:NSM], -1.0, both(gpar[:, 2 * VH:2 * VH + FH]), ALU.mult, ALU.subtract)
            o.after()
            ts(flat(sm), flat(sm2), -1.0, None, ALU.mult)
            o.after()
            tt(flat(sm), flat(sm), flat(sm2), ALU.min, "small_neg", 1)
            dve.wait_ge(N["small_exp"].sem, 1)
            ts(flat(log_s), flat(sm), 2.0, None, ALU.add)
            o.after()
            o.do(v.reciprocal(flat(log_s), flat(log_s)))
            o.after()
            tt(flat(log_s), flat(log_s), flat(sm), ALU.mult)
            o.after()
            tt(flat(log_s2), flat(log_s), flat(log_s), ALU.mult)
            o.after()
            ts(flat(sm), flat(log_s2), 1.0 / (2 * LOG_TERMS + 1), None, ALU.mult)
            for n in range(LOG_TERMS - 1, 0, -1):
                o.after()
                stt(flat(sm), flat(sm), 1.0 / (2 * n + 1), flat(log_s2), ALU.add, ALU.mult)
            o.after()
            stt(flat(sm), flat(sm), 1.0, flat(log_s), ALU.add, ALU.mult)
            o.after()
            ts(flat(sm), flat(sm), 2.0, None, ALU.mult)
            o.after()
            stt(flat(sm2), flat(sm2), 0.0, flat(sm), ALU.max, ALU.add, "small_sp", 1)
            o.after()
            stt(sm2[:, :, VH:2 * VH], sm2[:, :, VH:2 * VH], -1.0, both(gpar[:, 0:VH]), ALU.mult, ALU.mult)
            ts(sm2[:, :, 2 * VH:NSM], sm2[:, :, 2 * VH:NSM], -1.0, None, ALU.mult)
            o.after()
            dve.sem_inc(N["logs_made"].sem, 1)
            dve.wait_ge(N["sums_in"].sem, 1)
            tt(heads[:, 3, :, :], heads[:, 2, :, :], heads[:, 1, :, :], ALU.mult)
            tt(heads[:, 4, :, :], bank[1][:, MT * VH:2 * MT * VH].rearrange("p (m h) -> p m h", m=MT), heads[:, 0, :, :],
               ALU.subtract, "decay_left", 1)
            o.end()
            meet(dve, "dve", 3, o)

            for u in range(LEAD):
                lo_unit(u, u, u)

            with dve.Fori(0, NCH) as i:
                o.begin(i, 400)
                count = [0]
                next_slot = slots(i, MAIN_UNITS, 0, MAIN_RAW, R_MAIN, raw_place, count)

                def wait(name, k):
                    dve.wait_ge(N[name].sem, N[name].value(i, k))

                def until(job):
                    while count[0] < (job + 1) * KT:
                        next_slot()

                def taps(dst, srcs, w, ntap, sig_name, sig_k):
                    for n in range(ntap):
                        o.after()
                        for b in range(BPC):
                            tap = ntap - 1 - n
                            last = n == ntap - 1 and b == BPC - 1
                            args = (sig_name, sig_k) if last else (None, None)
                            if n == 0:
                                ts(dst[:, b, :], srcs(b), w(b, tap), None, ALU.mult, name=args[0], k=args[1])
                            else:
                                stt(dst[:, b, n:S], srcs(b)[:, 0:S - n], w(b, tap), dst[:, b, n:S], ALU.mult, ALU.add, *args)

                def mod_columns(n):
                    wait("mcol_done", n + 1)
                    at = i * (MODS * BPC) + (NMOD_FIRST + n) * BPC
                    tt(mod[:, bass.ds(at, BPC)], bank[0][:, 0:BPC], bada[:, bass.ds(at, BPC)], ALU.add, "mod_made", n + 1)

                def halves(n):
                    return lambda b: bank[n + b // 2][:, (b % 2) * S:(b % 2 + 1) * S]

                fence(dve, "dve", i, 1, o)
                copy(cur[:, :, :, :].rearrange("p a m h -> p (a m) h"),
                     heads[:, :, :, :].rearrange("p a m h -> p (a m) h")[:, :, bass.ds(i * VPC, VPC)])
                copy(cur_cd[:, :, :], cd[:, :, bass.ds(i * VPC, VPC)])
                copy(cur_f[:, :, :], fcum[:, :, bass.ds(i * KPC, KPC)])
                for s in range(3):
                    copy(cur_cwg[:, s, :, :], cwg[:, :, bass.ds(i * BPC + s * KT, BPC)])
                copy(cur_cwa[:, :, :], cwa[:, :, bass.ds(i * BPC, BPC)])
                for k, job in enumerate((J_GQ, J_GK, J_GV)):
                    until(job)
                    next_slot()
                    next_slot()
                    wait("turned", k + 1)
                    taps((QC, KC, VC)[k], halves(2 * (k % 2)), lambda b, tap: cur_cwg[:, k, tap, b:b + 1], TAPS_G, "conv_made", k + 1)
                    next_slot()
                until(J_GZ)
                next_slot()
                next_slot()
                next_slot()
                next_slot()
                wait("rn_made", 1)
                for n in range(4):
                    src = (QC, KC)[n // 2][:, 2 * (n % 2):2 * (n % 2) + 2, :].rearrange("p a b -> p (a b)")
                    tt(src, src, norm_tmp[n], ALU.mult, *(("qk_made", 1) if n == 3 else ()))
                next_slot()
                wait("tok_done", 2)
                for m in range(MT):
                    copy(vtok[:, m, :], bank[2 + m][:, :], *(("v_tok_in", 1) if m else ()))
                next_slot()
                fence(dve, "dve", i, 2, o)
                mod_columns(0)
                next_slot()

                def delta_pair(pair):
                    fence(dve, "dve", i, 3 + pair, o)
                    next_slot()
                    for e in range(2):
                        k = 2 * pair + e
                        wait("gb_done", k + 1)
                        for q in range(4):
                            t, r = divmod(q, 2)
                            ts(X[e]["V"][:, q, :], bank[2 + e][:, q * P:(q + 1) * P], cur[:, 0, t, 2 * k + r:2 * k + r + 1],
                               0.0, ALU.subtract, ALU.min, *(("d_made", k + 1) if q == 3 else ()))
                    for e in range(2):
                        k = 2 * pair + e
                        wait("kk_done", k + 1)
                        wait("decay_made", k + 1)

                        def over_heads(lo):
                            a = bank[e][:, lo:lo + MT * P].rearrange("p (t c) -> p t c", t=MT)
                            return a.unsqueeze(2).broadcast_to([P, MT, 2, P])

                        four = lambda t: t[:, :, :].rearrange("p (t r) c -> p t r c", r=2)
                        tt(four(X[e]["KB"]), over_heads(0), four(X[e]["V"]), ALU.mult, "low_made", k + 1)
                        tt(four(X[e]["IT"]), over_heads(MT * P), four(X[e]["V"]), ALU.mult, "it_made", k + 1)
                    next_slot()
                    next_slot()
                    for e in range(2):
                        k = 2 * pair + e
                        wait("b_made", pair * 2 * (LEVELS + 1) + e + 1)
                        tt(X[e]["T"][:, :, :], ident[:, :].unsqueeze(1).broadcast_to([P, 4, P]), X[e]["B"][:, :, :],
                           ALU.subtract, "t1_made", k + 1)
                    next_slot()
                    next_slot()
                    for l in range(LEVELS):
                        next_slot()
                        for e in range(2):
                            k = 2 * pair + e
                            n = pair * 2 * LEVELS + 2 * l + e + 1
                            wait("dtt_done", n)
                            if l == 0:
                                wait("tt1_made", k + 1)
                            tt(flat(X[e]["TT"]), flat(X[e]["TT"]), bank[2 if e == 0 else 0][:, :], ALU.subtract, "tt_made", n)
                            wait("dt_done", n)
                            tt(flat(X[e]["T"]), flat(X[e]["T"]), bank[3 if e == 0 else 1][:, :], ALU.subtract, "t_made", n)
                        next_slot()
                    for e in range(2):
                        k = 2 * pair + e
                        wait("u_done", k + 1)
                        copy(X[e]["UU"], bank[2 + e][:, 0:4 * DV].rearrange("p (a b) -> p a b", a=4), "uu_made", k + 1)
                    o.after()
                    next_slot()
                    for j in range(NCK):
                        t, h = divmod(j, 2)
                        rw = slice(CH * h, CH * h + CH)
                        first = pair * 2 * NCK + 2 * j + 1
                        for e in range(2):
                            x_ = X[e]
                            wait("ws_done", first + e)
                            tt(x_["VN"][rw, :], x_["UU"][rw, 2 * t:2 * t + 2, :].rearrange("p a b -> p (a b)"),
                               bank[e][rw, 0:P], ALU.subtract)
                        o.after()
                        for e in range(2):
                            k = 2 * pair + e
                            x_ = X[e]
                            tt(x_["VS"][rw, :].rearrange("p (a b) -> p a b", a=2), x_["VN"][rw, :].rearrange("p (a b) -> p a b", a=2),
                               cur[rw, 4, t, 2 * k:2 * k + 2].unsqueeze(2).broadcast_to([CH, 2, DV]), ALU.mult, "vs_made", first + e)
                        next_slot()
                        for e in range(2):
                            k = 2 * pair + e
                            x_ = X[e]
                            wait("su_done", first + e)
                            for r in range(2):
                                st = x_["ST"][:, r * DV:(r + 1) * DV]
                                stt(st, st, cur_cd[:, j, 2 * k + r:2 * k + r + 1], bank[2 + e][:, 2 * P + r * DV:2 * P + (r + 1) * DV],
                                    ALU.mult, ALU.add, *(("s_made", first + e) if r else ()))
                        for e in range(2):
                            k = 2 * pair + e
                            wait("in_done", first + e)
                            wait("o1_made", first + e)
                            tt(vtok[rw, t, k * P:(k + 1) * P], X[e]["O1"][rw, :], bank[e][rw, P:2 * P], ALU.add, "o_made", first + e)
                        next_slot()

                delta_pair(0)
                for n, job in enumerate((J_FQ, J_FK)):
                    until(job)
                    next_slot()
                    wait("f_turned", n + 1)
                    dst = (FQ, FK)[n]
                    for h in range(2):
                        copy(dst[:, 2 * h:2 * h + 2, :].rearrange("p a b -> p (a b)"), bank[2 * n + h][:, :], *(("f_made", n + 1) if h else ()))
                    if n == 1:
                        mod_columns(1)
                    next_slot()
                delta_pair(1)
                fence(dve, "dve", i, 5, o)
                for m in range(MT):
                    wait("osq_made", m + 1)
                    o.do(v.tensor_reduce(rms[:, m * VPC:(m + 1) * VPC], flat(osq[m]).rearrange("p (h d) -> p h d", d=DV),
                                         mybir.AxisListType.X, ALU.add), *((N["rms_in"], 1) if m else ()))
                until(J_FV)
                next_slot()
                wait("rms_out", 1)
                for m in range(MT):
                    o3 = vtok[:, m, :].rearrange("p (h d) -> p h d", d=DV)
                    tt(o3, o3, rms[:, m * VPC:(m + 1) * VPC].unsqueeze(2).broadcast_to([P, VPC, DV]), ALU.mult, *(("rms_used", 1) if m else ()))
                next_slot()
                wait("cum_done", 1)
                for f in range(KPC):
                    ck = bank[2 + f // 2][:, (f % 2) * S:(f % 2 + 1) * S]
                    stt(BI[:, f, 0:P], ck[:, 0:P], cur_f[:, 0, f:f + 1], causal_big[:, :], ALU.subtract, ALU.add)
                    ts(BI[:, f, P:2 * P], ck[:, 0:P], cur_f[:, 1, f:f + 1], None, ALU.subtract)
                    stt(BI[:, f, 2 * P:3 * P], ck[:, P:2 * P], cur_f[:, 1, f:f + 1], causal_big[:, :], ALU.subtract, ALU.add,
                        *(("bias_made", 1) if f == KPC - 1 else ()))
                next_slot()
                mod_columns(2)
                next_slot()
                wait("scores_done", 1)
                o.after()
                for f in range(KPC):
                    stt(SC[:, f, :], bank[f][:, 0:3 * P], float(P) ** -0.5, BI[:, f, :], ALU.mult, ALU.subtract)
                o.after()
                for f in range(KPC):
                    for t in range(MT):
                        o.do(v.tensor_reduce(fmax[:, 0, MT * f + t:MT * f + t + 1], SC[:, f, t * P:(1 + 2 * t) * P],
                                             mybir.AxisListType.X, ALU.max, negate=True),
                             *((N["fmax_made"], 1) if (f, t) == (KPC - 1, MT - 1) else ()))
                next_slot()
                wait("fexp_made", 1)
                o.do(v.reciprocal(fmax[:, 1, :], fmax[:, 1, :]))
                o.after()
                for f in range(KPC):
                    for t in range(MT):
                        s_ = SC[:, f, t * P:(1 + 2 * t) * P]
                        ts(s_, s_, fmax[:, 1, MT * f + t:MT * f + t + 1], None, ALU.mult,
                           name="prob_made" if (f, t) == (KPC - 1, MT - 1) else None, k=1)
                next_slot()
                next_slot()
                wait("yc_done", 1)
                for h in range(2):
                    for q in range(2):
                        copy(yT[2][:, bass.ds(i * BPC + 2 * h + q, 1), :].rearrange("p a b -> p (a b)"), bank[2 * h + q][:, 0:S])
                fence(dve, "dve", i, 6, o)
                until(J_CC)
                next_slot()
                wait("c_turned", 1)
                for h in range(2):
                    copy(FQ[:, 2 * h:2 * h + 2, :].rearrange("p a b -> p (a b)"), bank[h][:, :], *(("cc_made", 1) if h else ()))
                next_slot()
                until(J_CH)
                next_slot()
                wait("c_turned", 2)
                o.after()
                for h in range(2):
                    c2 = FQ[:, 2 * h:2 * h + 2, :].rearrange("p a b -> p (a b)")
                    tt(c2, c2, bank[2 + h][:, :], ALU.mult, *(("ch_made", 1) if h else ()))
                taps(FK, lambda b: FQ[:, b, :], lambda b, tap: cur_cwa[:, tap, b:b + 1], TAPS_A, "conv3_made", 1)
                next_slot()
                until(J_CB)
                next_slot()
                wait("c_turned", 3)
                for h in range(2):
                    tt(yT[0][:, bass.ds(i * BPC + 2 * h, 2), :].rearrange("p a b -> p (a b)"),
                       FK[:, 2 * h:2 * h + 2, :].rearrange("p a b -> p (a b)"), bank[h][:, :], ALU.mult, *(("ya_made", 1) if h else ()))
                mod_columns(3)
                next_slot()
                slots_made.append(count[0])
                o.end(NCH)
            o.begin(0, 4)
            ts(mod[:, 4 * KT:5 * KT], mod[:, 4 * KT:5 * KT], 1.0, None, ALU.add)
            o.end()
            meet(dve, "dve", 4, o)

            for b in range(3):
                for n in range(4):
                    dve.wait_ge(N["y_hi"].sem, 4 * b + n + 1)
                    tt(z_lo[:, 4 * n:4 * n + 4, :], yT[b][:, 4 * n:4 * n + 4, :], z_hi[:, 4 * n:4 * n + 4, :], ALU.subtract, "y_lo", 4 * b + n + 1)
                with dve.Fori(0, NCH) as i:
                    o.begin(i, 4)
                    count = [0]
                    next_slot = slots(i, 2 * UPJ, J_MERGE * UPJ + b * 2 * UPJ * NCH, 2 * UPJ,
                                      R_MERGE + b * 2 * UPJ * NCH, plain_place, count)
                    for _ in range(4 * UPJ):
                        next_slot()
                    j = J_MERGE + 2 * NCH * b
                    job_wait(dve, i * 2 + (j + 1))
                    dve.wait_ge(acc_free[0].sem, i + (j // 2 + 2))
                    mg = merged[:, :, bass.ds(i * NC, NC)]
                    if b:
                        o.do_count(v.tensor_tensor(gated[:, :, :], sig[:, :, :], acc[1][:, :, :], ALU.mult), acc_free[1].sem, i + (j // 2 + 2))
                        o.after()
                        tt(mg, mg, gated[:, :, :], ALU.add)
                    else:
                        o.do_count(v.tensor_tensor(mg, sig[:, :, :], acc[1][:, :, :], ALU.mult), acc_free[1].sem, i + (j // 2 + 2))
                        o.after()
                        copy(rstd[:, 0:1], eps_b[:, 0:1])
                    o.end(NCH)
            meet(dve, "dve", 5, o)
            for n in range(8):
                dve.wait_ge(N["z_hi_made"].sem, n + 1)
                tt(z_lo[:, 2 * n:2 * n + 2, :].rearrange("p a b -> p (a b)"), bank[n % 4][:, :],
                   z_hi[:, 2 * n:2 * n + 2, :].rearrange("p a b -> p (a b)"), ALU.subtract, "z_lo_made", n + 1)
            dve.wait_ge(N["gate_made"].sem, NCH)
            dve.wait_ge(ln_in.sem, 48)
            with dve.Fori(0, NCH // 2) as i:
                o.begin(i, 8)
                count = [0]
                next_slot = slots(i, 2 * UPJ, J_OUT * UPJ, 2 * UPJ, R_OUT, plain_place, count)
                for j in range(2):
                    while count[0] < (j + 1) * KT:
                        next_slot()
                    job_wait(dve, i * 2 + (J_OUT + j))
                    cols = bass.ds(i * (2 * NC) + j * NC, NC)
                    gb = gate_b[:, cols].unsqueeze(1).broadcast_to([P, MT, NC])
                    o.do_count(v.tensor_tensor(xr[:, :, cols], acc[j][:, :, :], gb, ALU.mult), acc_free[j].sem, i + (J_OUT // 2 + 2))
                    o.after()
                    stt(xr[:, :, cols], x1[:, :, cols], ALPHA, xr[:, :, cols], ALU.mult, ALU.add)
                o.end(NCH // 2)

            def layer_norm(which):
                for m in range(MT):
                    o.after()
                    for n in range(NCH):
                        o.do(v.bn_stats(stats[:, m, n, :], xr[:, m, n * NC:(n + 1) * NC]))
                    o.after()
                    o.do(v.bn_aggr(aggr[:, m, :], stats[:, m, :, :].rearrange("p a b -> p (a b)")), N["ln_var"], which * MT + m + 1)
                for m in range(MT):
                    dve.wait_ge(N["ln_rstd"].sem, which * MT + m + 1)
                    ts(xr[:, m, :], xr[:, m, :], aggr[:, m, 0:1], rstd[:, m:m + 1], ALU.subtract, ALU.mult)
                    o.after()
                    tt(xr[:, m, :], xr[:, m, :], ln_g[:, :], ALU.mult)
                    o.after()
                    tt(x1[:, m, :], xr[:, m, :], ln_b[:, :], ALU.add, "ln_ready", which * MT + m + 1)

            o.begin(0, 60)
            layer_norm(0)
            for n in range(8):
                dve.wait_ge(N["u2_hi"].sem, n + 1)
                tt(u_lo[:, 2 * n:2 * n + 2, :].rearrange("p a b -> p (a b)"), gated[:, n % 2, :],
                   u_hi[:, 2 * n:2 * n + 2, :].rearrange("p a b -> p (a b)"), ALU.subtract, "u2_lo", n + 1)
            o.do(v.memset(merged[:, :, :], 0.0))
            o.end()
            meet(dve, "dve", 6, o)
            with dve.Fori(0, FFQ) as i:
                o.begin(i, 20)
                count = [0]
                next_slot = slots(i, FF_JOBS * UPJ, J_FF * UPJ, FF_JOBS * UPJ, R_FF, plain_place, count)
                for j in range(NCH):
                    while count[0] < (j + 1) * KT:
                        next_slot()
                    next_slot()
                    next_slot()
                    dve.wait_ge(N["h_hi"].sem, N["h_hi"].value(i, j + 1))
                    for h in range(2):
                        tt(z_lo[:, 4 * j + 2 * h:4 * j + 2 * h + 2, :].rearrange("p a b -> p (a b)"), bank[2 * (j % 2) + h][:, :],
                           z_hi[:, 4 * j + 2 * h:4 * j + 2 * h + 2, :].rearrange("p a b -> p (a b)"), ALU.subtract, "h_lo", 2 * j + h + 1)
                for j in range(NCH, FF_JOBS):
                    while count[0] < (j + 1) * KT:
                        next_slot()
                    job_wait(dve, i * FF_JOBS + (J_FF + j))
                    mg = merged[:, :, (j - NCH) * NC:(j - NCH + 1) * NC]
                    o.do_count(v.tensor_tensor(mg, mg, acc[j % 2][:, :, :], ALU.add), acc_free[j % 2].sem,
                               i * (FF_JOBS // 2) + ((J_FF + j) // 2 + 2))
                o.after()
                copy(rstd[:, 0:1], eps_b[:, 0:1])
                o.end(FFQ)
            meet(dve, "dve", 7, o)
            o.begin(0, 60)
            tt(xr[:, :, :], merged[:, :, :], gate_b[:, :].unsqueeze(1).broadcast_to([P, MT, D]), ALU.mult)
            o.after()
            stt(xr[:, :, :], x1[:, :, :], ALPHA, xr[:, :, :], ALU.mult, ALU.add)
            dve.wait_ge(ln_in.sem, 80)
            layer_norm(1)
            o.after()

        @block.tensor
        def _(pe):
            t_ = nc.tensor

            def mm(dst, lhsT, rhs, start=True, stop=True):
                return t_.matmul(dst, lhsT, rhs, start=start, stop=stop)

            def turn(dst, src):
                return t_.transpose(dst, src, ident[:, :])

            def k_tile(n, u, q, dst, j, left):
                k = UK * (u % UPJ) + q
                hi, lo = left
                if q == 0:
                    pe.wait_ge(lo_ready.sem, n + 1)
                if k == 0:
                    pe.wait_ge(acc_free[dst].sem, j)
                sl = u % PARTS
                for m in range(MT):
                    ms = slice(m * P, (m + 1) * P)
                    mm(acc[dst][:, m, :], hi[:, k, ms], w_hi[:, sl, q, :], k == 0, False)
                    mm(acc[dst][:, m, :], hi[:, k, ms], w_lo[:, sl, q, :], False, False)
                    last = mm(acc[dst][:, m, :], lo[:, k, ms], w_hi[:, sl, q, :], False, k == KT - 1)
                if q == UK - 1:
                    last.then_inc(units_used.sem, 1)

            def slots(i, units, unit0, count, left):
                def go_on():
                    s = count[0]
                    count[0] += 1
                    if s < 2 * units:
                        job = s // KT
                        k_tile(i * units + (unit0 + s // 2), s // 2, s % 2, job % 2,
                               i * (units // UPJ // 2) + (unit0 // UPJ + job) // 2 + 1, left(job, s))
                return go_on

            def ident_up(n):
                return ident[:, :]

            pe.sem_inc(units_used.sem, PARTS)
            pe.sem_inc(acc_free[0].sem, 1)
            pe.sem_inc(acc_free[1].sem, 1)
            pe.wait_ge(p_in.sem, 16 * 9)
            pe.wait_ge(met["pool"].sem, 1)
            for n, (at, r) in enumerate(((0, 96), (96, 96), (192, 96), (288, 48), (336, KT))):
                last = t_.transpose(bank[0][:, at:at + r], rows[0:r, n, :], ident[0:r, 0:r])
            last.then_inc(N["rows_turned"].sem, 1)
            meet(pe, "pe", 1)
            with pe.Fori(0, NMOD_FIRST) as i:
                pe.wait_ge(N["macc_first"].sem, i + 1)
                pe.wait_ge(N["mod_first"].sem, i)
                for b in range(BPC):
                    last = mm(bank[0][:, b:b + 1], macc[:, 0, b * P:(b + 1) * P], ones[:, 0:1])
                last.then_inc(N["mcol_first"].sem, 1)
            pe.wait_ge(N["mod_first"].sem, NMOD_FIRST)
            pe.wait_ge(x_in.sem, 16)
            for n in range(8):
                if n >= 4:
                    pe.wait_ge(N["u_made"].sem, 2 * (n - 4) + 2)
                for q in range(2):
                    for m in range(MT):
                        k = 2 * n + q
                        last = turn(bank[n % 4][:, q * S + m * P:q * S + (m + 1) * P], x_sb[:, m, k * P:(k + 1) * P])
                last.then_inc(N["x_turned"].sem, 1)
            pe.wait_ge(N["u_made"].sem, KT)
            meet(pe, "pe", 2)
            pe.wait_ge(ws_in.sem, 32)
            for m in range(MT):
                for k in range(KT):
                    last = mm(bank[0][:, m * NSM:(m + 1) * NSM], uT[:, k, m * P:(m + 1) * P], ws[:, k, :], k == 0, k == KT - 1)
            last.then_inc(N["small_done"].sem, 1)
            pe.wait_ge(N["logs_made"].sem, 1)
            for m in range(MT):
                mm(bank[1][:, m * VH:(m + 1) * VH], chunk_upper[:, :], sm2[:, m, VH:2 * VH])
                mm(bank[1][:, (MT + m) * VH:(MT + m + 1) * VH], chunk_ones[:, :], sm2[:, m, VH:2 * VH])
                for h in range(2):
                    mm(bank[2][:, (2 * m + h) * VH:(2 * m + h + 1) * VH], half_rows[:, h, :], sm2[:, m, VH:2 * VH])
            mm(bank[3][:, 0:FH], upper[:, :], sm2[:, 0, 2 * VH:NSM])
            mm(bank[3][:, FH:2 * FH], ones[:, :], sm2[:, 0, 2 * VH:NSM], True, False)
            mm(bank[3][:, FH:2 * FH], upper[:, :], sm2[:, 1, 2 * VH:NSM], False, True).then_inc(N["sums_done"].sem, 1)
            meet(pe, "pe", 3)

            with pe.Fori(0, NCH) as i:
                count = [0]
                next_slot = slots(i, MAIN_UNITS, 0, count, lambda job, s: (u_hi, u_lo))

                def wait(name, k):
                    pe.wait_ge(N[name].sem, N[name].value(i, k))

                def until(job):
                    while count[0] < (job + 1) * KT:
                        next_slot()

                def wait_taken(job):
                    pe.wait_ge(acc_free[job % 2].sem, i * (len(MAIN_JOBS) // 2) + (job // 2 + 2))

                def turn_stage(b0, name, k):
                    for b in range(BPC):
                        for m in range(MT):
                            last = turn(bank[b0 + b // 2][:, (b % 2) * S + m * P:(b % 2) * S + (m + 1) * P],
                                        stage[:, m, b * P:(b + 1) * P])
                    last.then_inc(N[name].sem, 1)

                def mod_columns(n):
                    wait("macc_ready", n + 1)
                    for b in range(BPC):
                        last = mm(bank[0][:, b:b + 1], macc[:, n % 2, b * P:(b + 1) * P], ones[:, 0:1])
                    last.then_inc(N["mcol_done"].sem, 1)

                fence(pe, "pe", i, 1)
                for k, job in enumerate((J_GQ, J_GK, J_GV)):
                    until(job)
                    next_slot()
                    wait_taken(job)
                    if k == 2:
                        wait("conv_made", 1)
                    turn_stage(2 * (k % 2), "turned", k + 1)
                    next_slot()
                    next_slot()
                until(J_GZ)
                next_slot()
                next_slot()
                wait("sq_made", 1)
                wait("conv_made", 3)
                for n in range(4):
                    last = mm(bank[n][:, :], ones[:, :], norm_tmp[n])
                last.then_inc(N["ssq_done"].sem, 1)
                next_slot()
                next_slot()
                next_slot()
                wait("qk_made", 1)
                wait("silu_made", 3)
                for b in range(BPC):
                    for m in range(MT):
                        last = turn(bank[m][:, b * P:(b + 1) * P], KC[:, b, m * P:(m + 1) * P])
                last.then_inc(N["tok_done"].sem, 1)
                for b in range(BPC):
                    for m in range(MT):
                        last = turn(bank[2 + m][:, b * P:(b + 1) * P], VC[:, b, m * P:(m + 1) * P])
                last.then_inc(N["tok_done"].sem, 1)
                next_slot()
                fence(pe, "pe", i, 2)
                mod_columns(0)
                next_slot()

                def delta_pair(pair):
                    wait("mod_made", pair + 1)
                    fence(pe, "pe", i, 3 + pair)
                    for e in range(2):
                        k = 2 * pair + e
                        for q in range(4):
                            t, r = divmod(q, 2)
                            g_col = cur[:, 0, t, 2 * k + r:2 * k + r + 1].broadcast_to([P, P])
                            last = turn(bank[2 + e][:, q * P:(q + 1) * P], g_col)
                        last.then_inc(N["gb_done"].sem, 1)
                        for t in range(MT):
                            ts_ = slice(t * P, (t + 1) * P)
                            mm(bank[e][:, t * P:(t + 1) * P], KC[:, k, ts_], KC[:, k, ts_])
                            last = mm(bank[e][:, (MT + t) * P:(MT + t + 1) * P], KC[:, k, ts_], QC[:, k, ts_])
                        last.then_inc(N["kk_done"].sem, 1)
                    next_slot()
                    next_slot()
                    for e in range(2):
                        k = 2 * pair + e
                        wait("low_made", k + 1)
                        wait("it_made", k + 1)
                        for q in range(4):
                            last = turn(bank[e][:, q * P:(q + 1) * P], X[e]["KB"][:, q, :])
                        last.then_inc(N["low_turned"].sem, 1)
                    next_slot()
                    next_slot()
                    for e in range(2):
                        k = 2 * pair + e
                        wait("t1_made", k + 1)
                        for q in range(4):
                            last = turn(bank[2 + e][:, q * P:(q + 1) * P], X[e]["T"][:, q, :])
                        last.then_inc(N["t1_turned"].sem, 1)
                    next_slot()
                    for l in range(LEVELS):
                        for e in range(2):
                            k = 2 * pair + e
                            n = pair * 2 * LEVELS + 2 * l + e + 1
                            x_ = X[e]
                            wait("b_made", pair * 2 * (LEVELS + 1) + 2 * (l + 1) + e + 1)
                            if l == 0:
                                wait("tt1_made", k + 1)
                                wait("l_made", k + 1)
                            else:
                                wait("t_made", pair * 2 * LEVELS + 2 * l)
                            for q in range(4):
                                last = mm(bank[e][:, q * P:(q + 1) * P], x_["B"][:, q, :], x_["TT"][:, q, :])
                            last.then_inc(N["v_done"].sem, 1)
                        next_slot()
                        for e in range(2):
                            n = pair * 2 * LEVELS + 2 * l + e + 1
                            x_ = X[e]
                            wait("v_made", n if e == 0 else n)
                            if e == 1:
                                wait("v_made", n)
                            d1, d2 = (2, 3) if e == 0 else (0, 1)
                            for q in range(4):
                                last = mm(bank[d1][:, q * P:(q + 1) * P], x_["T"][:, q, :], x_["V"][:, q, :])
                            last.then_inc(N["dtt_done"].sem, 1)
                            for q in range(4):
                                last = mm(bank[d2][:, q * P:(q + 1) * P], x_["V"][:, q, :], x_["T"][:, q, :])
                            last.then_inc(N["dt_done"].sem, 1)
                        next_slot()
                    wait("t_made", pair * 2 * LEVELS + 2 * LEVELS)
                    for e in range(2):
                        k = 2 * pair + e
                        x_ = X[e]
                        wait("kb_made", k + 1)
                        for q in range(4):
                            last = mm(bank[e][:, q * P:(q + 1) * P], x_["KB"][:, q, :], x_["TT"][:, q, :])
                        last.then_inc(N["wt_done"].sem, 1)
                        wait("vb_made", k + 1)
                        for q in range(4):
                            last = mm(bank[2 + e][:, q * DV:(q + 1) * DV], x_["TT"][:, q, :], x_["VB"][:, q, :])
                        last.then_inc(N["u_done"].sem, 1)
                    next_slot()
                    for j in range(NCK):
                        t, h = divmod(j, 2)
                        rw = slice(CH * h, CH * h + CH)
                        first = pair * 2 * NCK + 2 * j + 1
                        for e in range(2):
                            k = 2 * pair + e
                            x_ = X[e]
                            if j == 0:
                                wait("wt_made", k + 1)
                                wait("uu_made", k + 1)
                                wait("s_zero", k + 1)
                            else:
                                wait("s_made", first + e - 2)
                                wait("o_made", first + e - 2)
                                wait("o1_made", first + e - 2)
                            for r in range(2):
                                last = mm(bank[e][rw, r * DV:(r + 1) * DV], x_["WT"][:, 2 * t + r, rw], x_["ST"][:, r * DV:(r + 1) * DV])
                            last.then_inc(N["ws_done"].sem, 1)
                            mm(bank[2 + e][rw, P:2 * P], QC[:, k, j * CH:(j + 1) * CH], x_["ST"][:, :]).then_inc(N["qs_done"].sem, 1)
                        next_slot()
                        for e in range(2):
                            k = 2 * pair + e
                            x_ = X[e]
                            wait("vs_made", first + e)
                            wait("o1_made", first + e)
                            if j == 0:
                                wait("it_masked", k + 1)
                            mm(bank[2 + e][:, 2 * P:3 * P], ktok[rw, t, k * P:(k + 1) * P], x_["VS"][rw, :]).then_inc(N["su_done"].sem, 1)
                            for r in range(2):
                                last = mm(bank[e][rw, P + r * DV:P + (r + 1) * DV], x_["IT"][rw, 2 * t + r, rw], x_["VN"][rw, r * DV:(r + 1) * DV])
                            last.then_inc(N["in_done"].sem, 1)
                        next_slot()

                delta_pair(0)
                for n, job in enumerate((J_FQ, J_FK)):
                    until(job)
                    next_slot()
                    wait_taken(job)
                    if n == 0:
                        wait("o_made", 2 * NCK)
                        wait("s_made", 2 * NCK)
                    turn_stage(2 * n, "f_turned", n + 1)
                    if n == 1:
                        wait("f_made", 1)
                        mod_columns(1)
                    next_slot()
                delta_pair(1)
                fence(pe, "pe", i, 5)
                until(J_FV)
                next_slot()
                next_slot()
                for f in range(KPC):
                    for t in range(MT):
                        last = turn(bank[2 + f // 2][:, (f % 2) * S + t * P:(f % 2) * S + (t + 1) * P],
                                    cur_f[:, t, f:f + 1].broadcast_to([P, P]))
                last.then_inc(N["cum_done"].sem, 1)
                wait("yb_tok", MT)
                for b in range(BPC):
                    for m in range(MT):
                        last = turn(bank[b // 2][:, (b % 2) * S + m * P:(b % 2) * S + (m + 1) * P], vtok[:, m, b * P:(b + 1) * P])
                last.then_inc(N["yb_turned"].sem, 1)
                next_slot()
                wait("yb_made", 1)
                mod_columns(2)
                next_slot()
                wait("mod_made", 3)
                wait("bias_made", 1)
                for f in range(KPC):
                    mm(bank[f][:, 0:P], FQ[:, f, 0:P], FK[:, f, 0:P])
                    last = mm(bank[f][:, P:3 * P], FQ[:, f, P:2 * P], FK[:, f, 0:2 * P])
                last.then_inc(N["scores_done"].sem, 1)
                next_slot()
                wait("prob_made", 1)
                for f in range(KPC):
                    for n in range(3):
                        last = turn(bank[f][:, n * P:(n + 1) * P], SC[:, f, n * P:(n + 1) * P])
                last.then_inc(N["prob_turned"].sem, 1)
                next_slot()
                wait("probT_made", 1)
                for f in range(KPC):
                    fs = slice(f * P, (f + 1) * P)
                    mm(bank[f][:, 0:P], FV[:, 0, fs], PT[:, f, 0:P])
                    mm(bank[f][:, P:2 * P], FV[:, 0, fs], PT[:, f, P:2 * P], True, False)
                    last = mm(bank[f][:, P:2 * P], FV[:, 1, fs], PT[:, f, 2 * P:3 * P], False, True)
                last.then_inc(N["yc_done"].sem, 1)
                next_slot()
                fence(pe, "pe", i, 6)
                for n, job in enumerate((J_CC, J_CH, J_CB)):
                    until(job)
                    next_slot()
                    wait_taken(job)
                    turn_stage(2 * (n % 2), "c_turned", n + 1)
                    next_slot()
                wait("ya_made", 1)
                mod_columns(3)
                slots_made.append(count[0])
            meet(pe, "pe", 4)

            def left_after(hi, lo, name, first, every, z_from):
                def left(job, s):
                    return hi, lo
                return left

            for b in range(3):
                with pe.Fori(0, NCH) as i:
                    count = [0]

                    def merge_left(job, s):
                        if job == 0:
                            return u_hi, u_lo
                        if s == KT:
                            pe.wait_ge(N["y_lo"].sem, 4 * b + 4)
                        return z_hi, z_lo

                    next_slot = slots(i, 2 * UPJ, J_MERGE * UPJ + b * 2 * UPJ * NCH, count, merge_left)
                    for _ in range(4 * UPJ):
                        next_slot()
            pe.wait_ge(acc_free[1].sem, J_OUT // 2 + 1)
            meet(pe, "pe", 5)
            for n in range(8):
                if n >= 4:
                    pe.wait_ge(N["z_lo_made"].sem, n - 3)
                for q in range(2):
                    k = 2 * n + q
                    for m in range(MT):
                        last = turn(bank[n % 4][:, q * S + m * P:q * S + (m + 1) * P], merged[:, m, k * P:(k + 1) * P])
                last.then_inc(N["z_turned"].sem, 1)

            def gate_rows(which, at):
                for n in range(NCH):
                    for b in range(BPC):
                        k = at + n * BPC + b
                        last = mm(bank[n][:, b * P:(b + 1) * P], mod[:, k:k + 1].broadcast_to([P, P]), ident[:, :])
                    last.then_inc(N["gate_done"].sem, 1)

            pe.wait_ge(N["z_lo_made"].sem, 8)
            gate_rows(0, 2 * KT)
            with pe.Fori(0, NCH // 2) as i:
                count = [0]
                next_slot = slots(i, 2 * UPJ, J_OUT * UPJ, count, lambda job, s: (z_hi, z_lo))
                for _ in range(4 * UPJ):
                    next_slot()
            pe.wait_ge(N["gate_made"].sem, NCH)
            for n in range(8):
                pe.wait_ge(N["ln_ready"].sem, MT)
                if n >= 4:
                    pe.wait_ge(N["x1_scaled"].sem, n - 3)
                for q in range(2):
                    k = 2 * n + q
                    for m in range(MT):
                        last = turn(bank[n % 4][:, q * S + m * P:q * S + (m + 1) * P], x1[:, m, k * P:(k + 1) * P])
                last.then_inc(N["x1_turned"].sem, 1)
            pe.wait_ge(N["x1_scaled"].sem, 8)
            gate_rows(1, 5 * KT)
            pe.wait_ge(N["u2_lo"].sem, 8)
            meet(pe, "pe", 6)
            with pe.Fori(0, FFQ) as i:
                count = [0]

                def ff_left(job, s):
                    if job < NCH:
                        return u_hi, u_lo
                    if job == NCH and s % 2 == 0:
                        pe.wait_ge(N["h_lo"].sem, N["h_lo"].value(i, (s - NCH * KT) // 2 + 1))
                    return z_hi, z_lo

                next_slot = slots(i, FF_JOBS * UPJ, J_FF * UPJ, count, ff_left)
                for j in range(FF_JOBS):
                    while count[0] < (j + 1) * KT:
                        next_slot()
                    if j < NCH:
                        next_slot()
                        pe.wait_ge(N["squared"].sem, N["squared"].value(i, j + 1))
                        for b in range(BPC):
                            for m in range(MT):
                                last = turn(bank[2 * (j % 2) + b // 2][:, (b % 2) * S + m * P:(b % 2) * S + (m + 1) * P],
                                            stage[:, m, b * P:(b + 1) * P])
                        last.then_inc(N["h_turned"].sem, 1)
            meet(pe, "pe", 7)


_INPUTS = ["x", "c", "w_ada", "b_ada", "w_in", "conv_w", "gdn_conv_w", "gdn_a_log", "gdn_dt_bias",
           "gdn_norm_w", "fox_f_bias", "w_branch_a", "w_branch_b", "w_branch_c", "w_o", "ln1_g", "ln1_b",
           "w_ff1", "w_ff2", "ln2_g", "ln2_b"]


def kernel(**inputs):
    import numpy as np
    import concourse.bacc as bacc
    from concourse.bass_utils import run_bass_kernel_spmd

    nc = bacc.Bacc("TRN2", target_bir_lowering=False, num_devices=1)
    arrays, args = {}, []
    for name in _INPUTS:
        arrays[f"in_{name}"] = np.ascontiguousarray(inputs[name])
        args.append(nc.dram_tensor(f"in_{name}", arrays[f"in_{name}"].shape, F32, kind="ExternalInput").ap())
    out = nc.dram_tensor("out_dram", (1, S, D), F32, kind="ExternalOutput").ap()
    layer_program(nc, *args, out)
    return run_bass_kernel_spmd(nc, [arrays], core_ids=[0]).results[0]["out_dram"]
```

```python
import concourse.bass as bass
from concourse import mybir
from contextlib import ExitStack
import math

F32 = mybir.dt.float32
F32R = mybir.dt.float32r
ALU = mybir.AluOpType
ACT = mybir.ActivationFunctionType

P = 128
S = 256
MT = S // P
D = 2048
KT = D // P
NC = 512
NCH = D // NC
BPC = NC // P
UK = 2
UPJ = KT // UK
RAWS = 4
PARTS = 4
FENCES = 4
LEAD = 3
DFF = 4 * D
VH = 32
DV = D // VH
CH = 64
NCK = S // CH
FH = 16
KPC = BPC
VPC = NC // DV
PAIRS = KPC // 2
LEVELS = 5
TAPS_A, TAPS_G = 3, 4
LN_EPS, NORM_EPS = 1e-5, 1e-6
LOG_TERMS = 8
ALPHA = 2.0 ** 0.25
BIG = 1e30
NMOD = 6 * NCH
NMOD_FIRST = 2 * NCH

OFF_CB, OFF_CC, OFF_CH = 0, D, 2 * D
OFF_GQ, OFF_GK, OFF_GV, OFF_GZ = 3 * D, 4 * D, 5 * D, 6 * D
OFF_BA = 7 * D
OFF_FQ = 7 * D + 2 * VH
OFF_FK, OFF_FV, OFF_F = OFF_FQ + D, OFF_FQ + 2 * D, OFF_FQ + 3 * D
OFF_MA = OFF_F + FH
NSM = 2 * VH + FH

MAIN_JOBS = (OFF_GQ, OFF_GK, OFF_GV, OFF_GZ, OFF_FQ, OFF_FK, OFF_FV, OFF_CC, OFF_CH, OFF_CB)
J_GQ, J_GK, J_GV, J_GZ, J_FQ, J_FK, J_FV, J_CC, J_CH, J_CB = range(10)
MAIN_UNITS = len(MAIN_JOBS) * UPJ
MODS = (NMOD - NMOD_FIRST) // NCH
MAIN_RAW = MAIN_UNITS + MODS * UPJ
MOD_AFTER = (*range(3, 11), 15, 16, 24, 25, *range(35, 43), *range(49, 61))
R_MAIN = NMOD_FIRST * UPJ
R_MERGE = R_MAIN + NCH * MAIN_RAW
R_OUT = R_MERGE + 3 * NCH * 2 * UPJ
R_FF = R_OUT + NCH * UPJ
J_MERGE = NCH * len(MAIN_JOBS)
J_OUT = J_MERGE + 3 * NCH * 2
J_FF = J_OUT + NCH
FFQ = DFF // D
FF_JOBS = 2 * NCH

MOD_BANK = (0, 0, 3, 3)


def mod_after(u):
    return MOD_AFTER.index(u) if u in MOD_AFTER else None


def raw_place(u):
    return u + sum(mod_after(v) is not None for v in range(min(u, MAIN_UNITS)))


def plain_place(u):
    return u


class Signal:

    def __init__(self, sem, per):
        self.sem, self.per, self.made = sem, per, 0

    def value(self, i, k):
        return i * self.per + k


class Order:

    def __init__(self, eng, sem):
        self.eng, self.sem, self.base, self.i, self.pad, self.n, self.last = eng, sem, 0, 0, 0, 0, None

    def begin(self, i, pad):
        self.i, self.pad, self.n, self.last = i, pad, 0, None

    def do(self, ins, sig=None, k=None):
        if sig is None:
            self.n += 1
            ins.then_inc(self.sem, 1)
            self.last = (self.sem, self.i * self.pad + (self.base + self.n))
        else:
            sig.made += 1
            ins.then_inc(sig.sem, 1)
            self.last = (sig.sem, sig.value(self.i, k))

    def do_count(self, ins, sem, value):
        ins.then_inc(sem, 1)
        self.last = (sem, value)

    def after(self):
        if self.last is not None:
            self.eng.wait_ge(self.last[0], self.last[1])
            self.last = None

    def end(self, passes=1):
        assert self.n <= self.pad, (self.n, self.pad)
        self.after()
        if self.n:
            self.eng.wait_ge(self.sem, self.i * self.pad + (self.base + self.n))
        if self.pad > self.n:
            self.eng.sem_inc(self.sem, self.pad - self.n)
        self.base += passes * self.pad
        self.i = 0


def layer_program(nc, x, c, w_ada, b_ada, w_in, conv_w, gdn_conv_w, gdn_a_log, gdn_dt_bias,
                  gdn_norm_w, fox_f_bias, w_branch_a, w_branch_b, w_branch_c, w_o, ln1_g, ln1_b,
                  w_ff1, w_ff2, ln2_g, ln2_b, out):
    ctx = ExitStack()
    with ctx:
        base = (nc.sbuf_base + 31) // 32 * 32
        top = [0]

        def sb(name, shape, dt=F32, at=None):
            size = (4 * math.prod(shape[1:]) + 31) // 32 * 32
            if at is None:
                at = top[0]
                top[0] += size
            assert base + at + size <= nc.sbuf_usable_end, (name, at, size, nc.sbuf_usable_end)
            return nc.alloc_sbuf_tensor_at(name, shape, dt, offset=base + at)

        def flat(t):
            return t[:, :, :].rearrange("p a b -> p (a b)")

        raw = sb("raw", [P, RAWS, UK, NC])
        w_hi = sb("w_hi", [P, PARTS, UK, NC], F32R)
        w_lo = sb("w_lo", [P, PARTS, UK, NC], F32R)
        u_hi = sb("u_hi", [P, KT, S], F32R)
        u_lo = sb("u_lo", [P, KT, S], F32R)
        y_at = top[0]
        yT = [sb(f"y_{b}_T", [P, KT, S]) for b in "abc"]
        ident = sb("ident", [P, P])
        ones = sb("ones", [P, P])
        upper = sb("upper", [P, P])
        chunk_upper = sb("chunk_upper", [P, P])
        level_mask = sb("level_mask", [P, LEVELS + 1, P])
        causal_big = sb("causal_big", [P, P])
        mod = sb("mod", [P, 6 * KT])
        bada = sb("bada", [P, 6 * KT])
        c_act = sb("c_act", [P, KT])
        lnc_at = top[0]
        top[0] += 4 * 2 * KT
        cwg = sb("cwg", [P, TAPS_G, 3 * KT])
        cwa = sb("cwa", [P, TAPS_A, KT])
        norm_w = sb("norm_w", [P, DV])
        heads = sb("heads", [P, 5, MT, VH])
        cd = sb("cd", [P, NCK, VH])
        fcum = sb("fcum", [P, MT, FH])
        cur = sb("cur", [P, 5, MT, VPC])
        cur_cd = sb("cur_cd", [P, NCK, VPC])
        cur_f = sb("cur_f", [P, MT, KPC])
        cur_cwg = sb("cur_cwg", [P, 3, TAPS_G, BPC])
        cur_cwa = sb("cur_cwa", [P, TAPS_A, BPC])
        eps_b = sb("eps_b", [P, 3])
        fmax = sb("fmax", [P, 2, MT * KPC])
        rms = sb("rms", [P, MT * VPC])
        macc = sb("macc", [P, 2, NC])
        stage = sb("stage", [P, MT, NC])
        chunk_ones = sb("chunk_ones", [P, P], at=top[0] - 4 * MT * NC)
        half_rows = sb("half_rows", [P, 2, P], at=top[0] - 4 * MT * NC + 4 * P)
        tmp_at = top[0]
        QC = sb("QC", [P, BPC, S])
        KC = sb("KC", [P, BPC, S])
        VC = sb("VC", [P, BPC, S])
        FV = VC[:, :, :].rearrange("p (m b) s -> p m (b s)", m=MT)
        SZ = sb("SZ", [P, MT, NC])
        ktok = sb("ktok", [P, MT, NC])
        vtok = sb("vtok", [P, MT, NC])
        FQ = sb("FQ", [P, BPC, S])
        FK = sb("FK", [P, BPC, S])
        X = [dict() for _ in range(2)]
        for e in range(2):
            for n in ("V", "KB", "IT", "L", "B", "T", "TT"):
                X[e][n] = sb(f"{n}{e}", [P, 4, P])
            X[e]["VB"] = X[e]["L"][:, 0:2, :].rearrange("p a (b c) -> p (a b) c", c=DV)
            X[e]["UU"] = X[e]["T"][:, 0:2, :].rearrange("p a (b c) -> p (a b) c", c=DV)
            X[e]["VN"] = X[e]["T"][:, 2, :]
            X[e]["VS"] = X[e]["T"][:, 3, :]
            X[e]["WT"] = X[e]["B"]
            X[e]["ST"] = sb(f"ST{e}", [P, P])
            X[e]["O1"] = X[e]["V"][:, 0, :]
        at0 = top[0] - 4 * (2 * (7 * 4 * P + P))
        SC = sb("SC", [P, KPC, 3 * P], at=at0)
        BI = sb("BI", [P, KPC, 3 * P], at=at0 + 4 * KPC * 3 * P)
        PT = sb("PT", [P, KPC, 3 * P], at=at0 + 8 * KPC * 3 * P)
        osq = [X[1]["T"], X[1]["TT"]]
        norm_tmp = [flat(X[e][n]) for n in ("B", "T") for e in range(2)]
        x_sb = sb("x_sb", [P, MT, D], at=y_at)
        uT = sb("uT", [P, KT, S], at=y_at + 16384)
        ws = sb("ws", [P, KT, NSM], at=y_at + 32768)
        sm = sb("sm", [P, MT, NSM], at=y_at + 38000 // 32 * 32)
        sm2 = sb("sm2", [P, MT, NSM], at=y_at + 38688)
        rows = sb("rows", [P, 5, P], at=y_at + 39360)
        lnc = sb("lnc", [P, 2, KT], at=lnc_at)
        log_s = sb("log_s", [P, MT, NSM], at=tmp_at)
        log_s2 = sb("log_s2", [P, MT, NSM], at=tmp_at + 4 * MT * NSM)
        gpar = sb("gpar", [P, 2 * VH + FH], at=y_at + 41984)
        z_hi = sb("z_hi", [P, KT, S], F32R, at=tmp_at)
        z_lo = sb("z_lo", [P, KT, S], F32R, at=tmp_at + 16384)
        merged = sb("merged", [P, MT, D], at=tmp_at + 32768)
        sig = sb("sig", [P, MT, NC], at=tmp_at + 49152)
        gated = sb("gated", [P, MT, NC], at=tmp_at + 53248)
        x1 = sb("x1", [P, MT, D], at=y_at)
        xr = sb("xr", [P, MT, D], at=y_at + 16384)
        gate_b = sb("gate_b", [P, D], at=y_at + 32768)
        ln_g = sb("ln_g", [P, D], at=y_at + 40960)
        ln_b = sb("ln_b", [P, D], at=tmp_at + 49152)
        gate2_b = sb("gate2_b", [P, D], at=tmp_at + 32768)
        ff_part = sb("ff_part", [P, MT, NC], at=tmp_at + 32768 + 8192)
        stats = sb("stats", [P, MT, NCH, 6], at=tmp_at + 57344)
        aggr = sb("aggr", [P, MT, 2], at=tmp_at + 57344 + 256)
        rstd = sb("rstd", [P, MT], at=tmp_at + 57344 + 288)

        acc = [ctx.enter_context(nc.psum_tensor(f"acc{p}", [P, MT, NC], F32)) for p in range(2)]
        bank = [ctx.enter_context(nc.psum_tensor(f"bank{p}", [P, NC], F32)) for p in range(4)]

        def signal(name, per=1):
            return Signal(ctx.enter_context(nc.semaphore(name)), per)

        raw_ready = [signal(f"raw_ready{s}") for s in range(RAWS)]
        raw_free, hi_ready, lo_ready, units_used = (
            signal(n) for n in ("raw_free", "hi_ready", "lo_ready", "units_used"))
        acc_free = [signal(f"acc_free{p}") for p in range(2)]
        own = {n: ctx.enter_context(nc.semaphore(f"{n}_order")) for n in ("act", "dve", "pool")}
        met = {n: signal(f"{n}_met") for n in ("pe", "act", "dve", "pool")}
        c_in, x_in, p_in, g_in, ws_in, ln_in, stored, slots_granted = (
            signal(n) for n in ("c_in", "x_in", "p_in", "g_in", "ws_in", "ln_in", "stored", "slots_granted"))
        N = {}
        for name, per in dict(
                ident_made=1, masks_made=1, c_turned_in=1, c_made=1, x_turned=1, x_copied=1, rows_turned=1, rows_in=1,
                macc_first=1, mcol_first=1, mod_first=1, u_even=1, u_odd=1,
                u_hi_made=1, u_lo_made=1, small_done=1, small_in=1, small_neg=1, small_exp=1, small_sp=1, logs_made=1,
                sums_done=1, sums_in=1, decay_left=1, ln_var=1, ln_rstd=1, out_made=1,
                macc_ready=MODS, mcol_done=MODS, mod_made=MODS,
                turned=3, cur_made=1, tap_made=3, conv_made=3, silu_made=3, sq_made=1, ssq_done=1, rn_made=1, qk_made=1,
                tok_done=2, k_tok_in=1, v_tok_in=1,
                kk_done=4, gb_done=4, d_made=4, decay_made=4, low_made=4, it_made=4, it_masked=4,
                low_turned=4, l_made=4, b_made=4 * (LEVELS + 1), t1_made=4, t1_turned=4, tt1_made=4,
                v_done=4 * LEVELS, v_made=4 * LEVELS, d_done=4 * LEVELS,
                tt_made=4 * LEVELS, t_made=4 * (LEVELS - 1), kb_made=4, vb_made=4,
                wt_done=4, wt_made=4, u_done=4, uu_made=4,
                ws_done=4 * NCK, qs_done=4 * NCK, vs_made=4 * NCK, o1_made=4 * NCK,
                in_done=4 * NCK, su_done=4 * NCK, s_made=4 * NCK, s_zero=4, o_made=4 * NCK,
                osq_made=MT, rms_in=1, rms_out=1, rms_used=1, yb_tok=MT, yb_turned=1, yb_made=1,
                f_turned=2, f_made=2, cum_done=1, bias_made=1, scores_done=1, fmax_made=1,
                scored=1, fexp_made=1, finv_made=1, prob_made=1, prob_turned=1, probT_made=1, yc_done=1, yc_made=1,
                c_turned=3, cc_made=1, ch_made=1, conv3_made=1, ya_made=1,
                y_hi=1, y_lo=1, z_turned=1, z_hi_made=1, z_lo_made=1, gate_done=1, gate_made=1,
                merged_made=1, ln_scaled=1, xhat_made=1, xhat_turned=1, u2_even=1, u2_odd=1, u2_hi=1, u2_lo=1,
                base_made=1, squared=NCH, h_turned=NCH, h_hi=NCH, h_lo=UPJ).items():
            N[name] = signal(name, per)
        fences = {n: signal(f"{n}_fence", FENCES) for n in ("pe", "act", "dve", "pool")}

        block = ctx.enter_context(nc.Block())

        w_in_t = w_in[0].rearrange("(k p) n -> p k n", p=P)
        w_ada_t = w_ada[0].rearrange("(k p) n -> p k n", p=P)
        w_br_t = [w[0].rearrange("(k p) n -> p k n", p=P) for w in (w_branch_a, w_branch_b, w_branch_c)]
        w_o_t = w_o[0].rearrange("(k p) n -> p k n", p=P)
        w_ff1_t = w_ff1[0].rearrange("(k p) n -> p k n", p=P)
        w_ff2_t = w_ff2[0].rearrange("(k p) n -> p k n", p=P)

        def meet(eng, me, n, order=None):
            if order is not None:
                order.after()
            eng.sem_inc(met[me].sem, 1)
            for other in met:
                if other != me:
                    eng.wait_ge(met[other].sem, n)

        def fence(eng, me, i, n, order=None, meanwhile=None):
            if order is not None:
                order.after()
            eng.sem_inc(fences[me].sem, 1)
            if meanwhile is not None:
                meanwhile()
            for other in fences:
                if other != me:
                    eng.wait_ge(fences[other].sem, fences[other].value(i, n))

        def halves_of(t, l, which):
            return t[:, :, :].rearrange("p q (b h c) -> p q b h c", h=2, c=2 << l)[:, :, :, which, :]

        def d_halves(e, which, l):
            packed = bank[2 + e][:, which * 4 * CH:(which + 1) * 4 * CH]
            return packed.rearrange("p (q b c) -> p q b c", q=4, c=2 << l)

        def d_half(e, which, q, l):
            return d_halves(e, which, l)[:, q]

        def u2(g, which):
            t = stage[:, g % 2, :]
            return t.rearrange("p (a b) -> p a b", a=2) if which == 2 else t[:, which * S:(which + 1) * S]

        def job_wait(eng, j):
            eng.wait_ge(units_used.sem, j * UPJ + (PARTS + UPJ))

        @block.sync
        def _(sp):
            def load(r, rl, src, k0, col):
                if not isinstance(col, int):
                    col = sp.snap(col)
                if not isinstance(k0, int):
                    k0 = sp.snap(k0)
                sp.wait_ge(raw_free.sem, r + 1)
                sp.sem_inc(slots_granted.sem, 1)
                sp.dma_start(raw[:, rl % RAWS, :, :], src[:, bass.ds(k0, UK), bass.ds(col, NC)]
                             ).then_inc(raw_ready[rl % RAWS].sem, 16)

            with sp.Fori(0, NMOD_FIRST) as i:
                for u in range(UPJ):
                    load(i * UPJ + u, u, w_ada_t, UK * u, i * NC)
            with sp.Fori(0, NCH) as i:
                r = 0
                for u in range(MAIN_UNITS):
                    load(i * MAIN_RAW + (R_MAIN + r), r, w_in_t, UK * (u % UPJ), i * NC + MAIN_JOBS[u // UPJ])
                    r += 1
                    m = mod_after(u)
                    if m is not None:
                        load(i * MAIN_RAW + (R_MAIN + r), r, w_ada_t, UK * (m % UPJ),
                             i * (MODS * NC) + (NMOD_FIRST + m // UPJ) * NC)
                        r += 1
            for b in range(3):
                with sp.Fori(0, NCH) as i:
                    for u in range(2 * UPJ):
                        src, col = (w_in_t, i * NC + (OFF_MA + b * D)) if u < UPJ else (w_br_t[b], i * NC)
                        load(i * (2 * UPJ) + (R_MERGE + b * NCH * 2 * UPJ + u), u, src, UK * (u % UPJ), col)
            with sp.Fori(0, NCH // 2) as i:
                for u in range(2 * UPJ):
                    load(i * (2 * UPJ) + (R_OUT + u), u, w_o_t, UK * (u % UPJ), i * (2 * NC) + u // UPJ * NC)
            with sp.Fori(0, FFQ) as q:
                for j in range(FF_JOBS):
                    for u in range(UPJ):
                        r = q * (FF_JOBS * UPJ) + (R_FF + j * UPJ + u)
                        if j < NCH:
                            load(r, u, w_ff1_t, UK * u, q * D + j * NC)
                        else:
                            load(r, u, w_ff2_t, q * KT + UK * u, (j - NCH) * NC)
            for u in range(LEAD):
                load(R_FF + FFQ * FF_JOBS * UPJ + u, u, w_ff1_t, UK * u, 0)
            for m in range(MT):
                sp.wait_ge(N["out_made"].sem, m + 1)
                sp.dma_start(out[0, m * P:(m + 1) * P, :], x1[:, m, :]).then_inc(stored.sem, 16)
            sp.wait_ge(stored.sem, 16 * MT)

        @block.gpsimd
        def _(pool):
            o = Order(pool, own["pool"])
            g = nc.gpsimd
            o.begin(0, 60)
            o.do(g.memset(ident[:, :], 0.0))
            o.after()
            o.do(g.affine_select(out=ident[:, :], in_=ident[:, :], compare_op=ALU.not_equal, fill=1.0, base=0,
                                 pattern=[[-1, P]], channel_multiplier=1), N["ident_made"], 1)
            for t, v in ((ones, 1.0), (upper, 1.0), (chunk_upper, 1.0), (chunk_ones, 1.0)):
                o.do(g.memset(t[:, :], v))
            o.do(g.memset(half_rows[:, :, :], 1.0))
            o.do(g.memset(level_mask[:, :, :], 0.0))
            o.do(g.memset(causal_big[:, :], 0.0))
            for n, v in enumerate((NORM_EPS, -0.5 * math.log(P), LN_EPS)):
                o.do(g.memset(eps_b[:, n:n + 1], v))
            o.after()

            def keep(t, pattern, start, cm, fill=0.0, op=ALU.is_ge):
                o.do(g.affine_select(out=t, in_=t, compare_op=op, fill=fill, base=start, pattern=pattern,
                                     channel_multiplier=cm))
                o.after()

            keep(upper[:, :], [[1, P]], 0, -1)
            for t in (chunk_upper, chunk_ones):
                v = t[:, :].rearrange("p (b c) -> p b c", c=CH)
                keep(v, [[-CH, 2], [0, CH]], 0, 1)
                keep(v, [[CH, 2], [0, CH]], CH - 1, -1)
            keep(chunk_upper[:, :], [[1, P]], 0, -1)
            keep(half_rows[:, 0, :], [[0, P]], CH - 1, -1)
            keep(half_rows[:, 1, :], [[0, P]], -CH, 1)
            keep(causal_big[:, :], [[-1, P]], 0, 1, BIG)
            for l in range(LEVELS + 1):
                s = 1 << l
                v = level_mask[:, l, :].rearrange("p (b h c) -> p b h c", h=2, c=s)[:, :, 0, :]
                o.do(g.memset(v, 1.0))
                o.after()
                keep(v, [[-2 * s, P // (2 * s)], [0, s]], -s, 1)
                keep(v, [[2 * s, P // (2 * s)], [0, s]], 2 * s - 1, -1)
            o.end()
            pool.sem_inc(N["masks_made"].sem, 1)

            with pool.Fori(0, NCH) as i:
                o.begin(i, 40)

                def wait(name, k):
                    pool.wait_ge(N[name].sem, N[name].value(i, k))

                fence(pool, "pool", i, 1, o)
                for pair in range(PAIRS):
                    fence(pool, "pool", i, 2 + pair, o)
                    for e in range(2):
                        k = 2 * pair + e
                        xe = X[e]

                        def scale_by(n, width):
                            return cur[:, n, :, 2 * k:2 * k + 2].unsqueeze(3).broadcast_to([P, MT, 2, width])

                        wait("l_made", k + 1)
                        mask = [level_mask[:, l, :].unsqueeze(1).broadcast_to([P, 4, P]) for l in range(LEVELS + 1)]
                        o.do(g.tensor_tensor(xe["B"][:, :, :], xe["L"][:, :, :], mask[0], ALU.mult),
                             N["b_made"], pair * 12 + e + 1)
                        o.do(g.memset(xe["ST"][:, :], 0.0), N["s_zero"], k + 1)
                    for e in range(2):
                        k = 2 * pair + e
                        xe = X[e]
                        wait("it_made", k + 1)
                        o.do(g.tensor_tensor(xe["IT"][:, :, :], xe["IT"][:, :, :],
                                             chunk_upper[:, :].unsqueeze(1).broadcast_to([P, 4, P]), ALU.mult),
                             N["it_masked"], k + 1)
                    for l in range(LEVELS):
                        for e in range(2):
                            k = 2 * pair + e
                            xe = X[e]
                            if l == 0:
                                wait("t1_made", k + 1)
                            else:
                                wait("v_done", pair * 2 * LEVELS + 2 * (l - 1) + e + 1)
                            o.do(g.tensor_tensor(xe["B"][:, :, :], xe["L"][:, :, :], mask[l + 1], ALU.mult),
                                 N["b_made"], pair * 12 + 2 * (l + 1) + e + 1)
                            if l == 1:
                                kk = ktok[:, :, k * P:(k + 1) * P].unsqueeze(2).broadcast_to([P, MT, 2, P])
                                o.do(g.tensor_tensor(xe["KB"][:, :, :].rearrange("p (t r) c -> p t r c", r=2), kk,
                                                     cur[:, 3, :, 2 * k:2 * k + 2].unsqueeze(3).broadcast_to([P, MT, 2, P]),
                                                     ALU.mult), N["kb_made"], k + 1)
                    for e in range(2):
                        k = 2 * pair + e
                        xe = X[e]
                        pool.wait_ge(N["b_made"].sem, N["b_made"].value(i, pair * 12 + 12))
                        vv = vtok[:, :, k * P:(k + 1) * P].rearrange("p t (r c) -> p t r c", r=2)
                        o.do(g.tensor_tensor(xe["VB"].rearrange("p (t r) c -> p t r c", r=2), vv,
                                             cur[:, 2, :, 2 * k:2 * k + 2].unsqueeze(3).broadcast_to([P, MT, 2, DV]),
                                             ALU.mult), N["vb_made"], k + 1)
                fence(pool, "pool", i, 4, o)
                for m in range(MT):
                    o.do(g.tensor_tensor(flat(osq[m]), vtok[:, m, :], vtok[:, m, :], ALU.mult), N["osq_made"], m + 1)
                nw = norm_w[:, :].unsqueeze(1).broadcast_to([P, VPC, DV])
                for m in range(MT):
                    z = SZ[:, m, :].rearrange("p (h d) -> p h d", d=DV)
                    o.do(g.tensor_tensor(z, z, nw, ALU.mult))
                o.after()
                wait("rms_used", 1)
                for m in range(MT):
                    o.do(g.tensor_tensor(vtok[:, m, :], vtok[:, m, :], SZ[:, m, :], ALU.mult), N["yb_tok"], m + 1)
                o.end(NCH)
            meet(pool, "pool", 1, o)
            pool.wait_ge(N["ln_scaled"].sem, 1)
            pool.wait_ge(N["xhat_made"].sem, NCH)
            pool.wait_ge(N["xhat_turned"].sem, KT)
            o.begin(0, 10)
            for m in range(MT):
                o.do(g.tensor_tensor(xr[:, m, :], x1[:, m, :], ln_g[:, :], ALU.mult))
            o.after()
            for m in range(MT):
                o.do(g.tensor_tensor(xr[:, m, :], xr[:, m, :], ln_b[:, :], ALU.add), *((N["base_made"], 1) if m else ()))
            o.end()

        @block.scalar
        def _(act):
            o = Order(act, own["act"])
            a = nc.scalar

            def activate(dst, src, func, name=None, k=None, **kw):
                o.do(a.activation(dst, src, func, **kw), N[name] if name else None, k)

            def hi_unit(n, u, r, rl):
                act.wait_ge(raw_ready[rl % RAWS].sem, r)
                act.wait_ge(units_used.sem, n + 1)
                a.activation(w_hi[:, u % PARTS, :, :], raw[:, rl % RAWS, :, :], ACT.Copy).then_inc(hi_ready.sem, 1)

            def slots(i, units, unit0, raws, raw0, place, count):
                def one():
                    s = count[0]
                    count[0] += 1
                    if s % 2 and s // 2 < units:
                        u = s // 2 + LEAD
                        rl = place(u)
                        hi_unit(i * units + (unit0 + u), u, i * (16 * raws // RAWS) + 16 * ((raw0 + rl) // RAWS + 1), rl)

                def go_on(times=1):
                    for _ in range(times):
                        one()
                return go_on

            act.dma_start(rows[0:KT, 4, :], c[0].rearrange("(r p) -> r p", p=P)).then_inc(c_in.sem, 16)
            act.dma_start(x_sb[:, :, :], x[0].rearrange("(m p) n -> p m n", p=P)).then_inc(x_in.sem, 16)
            act.dma_start(rows[0:6 * KT, 0, :], b_ada[0].rearrange("(r p) -> r p", p=P)).then_inc(p_in.sem, 16)
            for n, src in enumerate((ln1_g, ln1_b)):
                act.dma_start(rows[KT * (n + 1):KT * (n + 2), 4, :], src[0].rearrange("(r p) -> r p", p=P)).then_inc(p_in.sem, 16)
            taps_rows = gdn_conv_w[0].rearrange("w (r p) -> (w r) p", p=P)
            for h in range(2):
                act.dma_start(rows[0:96, 1 + h, :], taps_rows[96 * h:96 * h + 96, :]).then_inc(p_in.sem, 16)
            act.dma_start(rows[0:TAPS_A * KT, 3, :], conv_w[0].rearrange("w (r p) -> (w r) p", p=P)).then_inc(p_in.sem, 16)
            for at, n, src in ((0, VH, gdn_a_log), (VH, VH, gdn_dt_bias), (2 * VH, FH, fox_f_bias)):
                act.dma_start(gpar[:, at:at + n], src[0].partition_broadcast(P)).then_inc(g_in.sem, 16)
            act.dma_start(norm_w[:, :], gdn_norm_w[0].partition_broadcast(P)).then_inc(g_in.sem, 16)
            act.dma_start(ws[:, :, 0:2 * VH], w_in_t[:, :, OFF_BA:OFF_BA + 2 * VH]).then_inc(ws_in.sem, 16)
            act.dma_start(ws[:, :, 2 * VH:NSM], w_in_t[:, :, OFF_F:OFF_F + FH]).then_inc(ws_in.sem, 16)
            o.begin(0, 60)
            act.wait_ge(N["c_turned_in"].sem, 1)
            activate(c_act[:, :], bank[1][:, 0:KT], ACT.Silu, "c_made", 1)
            for n in range(8):
                act.wait_ge(N["x_turned"].sem, n + 1)
                activate(uT[:, 2 * n:2 * n + 2, :].rearrange("p a b -> p (a b)"), bank[2 + n % 2][:, :], ACT.Copy, "x_copied", n + 1)
            act.wait_ge(N["rows_turned"].sem, 1)
            activate(bada[:, :], bank[0][:, 0:96], ACT.Copy)
            activate(flat(cwg), bank[0][:, 96:288], ACT.Copy)
            activate(flat(cwa), bank[0][:, 288:336], ACT.Copy)
            activate(flat(lnc), bank[0][:, 336 + KT:336 + 3 * KT], ACT.Copy)
            o.after()
            act.sem_inc(N["rows_in"].sem, 1)
            act.wait_ge(N["mod_first"].sem, 1)

            def make_hi(g):
                act.wait_ge(N["u_odd"].sem, g + 1)
                act.wait_ge(N["u_even"].sem, g + 1)
                activate(u_hi[:, 2 * g:2 * g + 2, :], uT[:, 2 * g:2 * g + 2, :], ACT.Copy, "u_hi_made", g + 1)

            for g in range(KT // 2):
                k = 2 * g
                activate(uT[:, k, :], uT[:, k, :], ACT.Identity, "u_even", g + 1,
                         scale=mod[:, KT + k:KT + k + 1], bias=mod[:, k:k + 1])
                if g:
                    make_hi(g - 1)
            make_hi(KT // 2 - 1)
            for u in range(LEAD):
                hi_unit(u, u, 16 * ((R_MAIN + u) // RAWS + 1), u)
            act.wait_ge(g_in.sem, 16 * 4)
            activate(gpar[:, 0:VH], gpar[:, 0:VH], ACT.Exp)
            act.wait_ge(N["small_done"].sem, 1)
            for m in range(MT):
                activate(sm[:, m, :], bank[2 + m][:, 0:NSM], ACT.Copy, *(("small_in", 1) if m else ()))
            act.wait_ge(N["small_neg"].sem, 1)
            activate(flat(sm), flat(sm), ACT.Exp, "small_exp", 1)
            act.wait_ge(N["small_sp"].sem, 1)
            activate(heads[:, 2, :, :], sm2[:, :, 0:VH], ACT.Exp, scale=-1.0)
            act.wait_ge(N["sums_done"].sem, 1)
            decay_sums = bank[1][:, 0:MT * VH].rearrange("p (m h) -> p m h", m=MT)
            activate(heads[:, 0, :, :], decay_sums, ACT.Copy)
            activate(heads[:, 1, :, :], decay_sums, ACT.Exp)
            activate(flat(cd), bank[2][:, 0:NCK * VH], ACT.Exp)
            activate(flat(fcum), bank[3][:, 0:MT * FH], ACT.Copy, "sums_in", 1)
            act.wait_ge(N["decay_left"].sem, 1)
            activate(heads[:, 4, :, :], heads[:, 4, :, :], ACT.Exp)
            o.end()

            with act.Fori(0, NCH) as i:
                o.begin(i, 90)
                count = [0]
                next_slot = slots(i, MAIN_UNITS, 0, MAIN_RAW, R_MAIN, raw_place, count)

                def wait(name, k):
                    act.wait_ge(N[name].sem, N[name].value(i, k))

                def until(job):
                    while count[0] < (job + 1) * KT:
                        next_slot()

                def take_job(job, dst, func=ACT.Copy):
                    until(job)
                    job_wait(act, i * len(MAIN_JOBS) + job)
                    o.do_count(a.activation(dst, acc[job % 2][:, :, :], func),
                               acc_free[job % 2].sem, i * (len(MAIN_JOBS) // 2) + (job // 2 + 2))

                fence(act, "act", i, 1, o)
                for k, job in enumerate((J_GQ, J_GK, J_GV)):
                    if k:
                        wait("turned", k)
                    take_job(job, stage[:, :, :])
                    next_slot(2)
                    dst = (QC, KC, VC)[k]
                    wait("turned", k + 1)
                    wait("cur_made", 1)
                    for b in range(BPC):
                        activate(dst[:, b, :], bank[2 * (k % 2) + b // 2][:, (b % 2) * S:(b % 2 + 1) * S], ACT.Copy,
                                 *(("tap_made", k + 1) if b == BPC - 1 else ()), scale=cur_cwg[:, k, TAPS_G - 1, b:b + 1])
                    next_slot(7)
                    next_slot()
                    wait("conv_made", k + 1)
                    activate(dst[:, :, :], dst[:, :, :], ACT.Silu, "silu_made", k + 1)
                    if k == 1:
                        o.after()
                        for n in range(4):
                            src = (QC, KC)[n // 2][:, 2 * (n % 2):2 * (n % 2) + 2, :]
                            activate(norm_tmp[n], src.rearrange("p a b -> p (a b)"), ACT.Square, *(("sq_made", 1) if n == 3 else ()))
                        next_slot(3)
                        wait("ssq_done", 1)
                        for n in range(4):
                            activate(norm_tmp[n], bank[n][:, :], ACT.Ln, bias=eps_b[:, 0:1])
                        next_slot(2)
                        o.after()
                        for n in range(4):
                            kw = dict(bias=eps_b[:, 1:2]) if n < 2 else {}
                            activate(norm_tmp[n], norm_tmp[n], ACT.Exp, *(("rn_made", 1) if n == 3 else ()), scale=-0.5, **kw)
                next_slot(4)
                wait("tok_done", 1)
                for m in range(MT):
                    activate(ktok[:, m, :], bank[m][:, :], ACT.Copy, *(("k_tok_in", 1) if m else ()))
                wait("tok_done", 2)
                for m in range(MT):
                    activate(vtok[:, m, :], bank[2 + m][:, :], ACT.Copy, *(("v_tok_in", 1) if m else ()))
                next_slot(2)
                next_slot()

                def delta_pair(pair):
                    fence(act, "act", i, 2 + pair, o, next_slot)
                    for e in range(2):
                        k = 2 * pair + e
                        wait("d_made", k + 1)
                        activate(X[e]["V"][:, :, :], X[e]["V"][:, :, :], ACT.Exp, "decay_made", k + 1)
                    next_slot(2)
                    for e in range(2):
                        k = 2 * pair + e
                        wait("low_turned", k + 1)
                        for q in range(4):
                            t, r = divmod(q, 2)
                            activate(X[e]["L"][:, q, :], bank[e][:, q * P:(q + 1) * P], ACT.Copy,
                                     *(("l_made", k + 1) if q == 3 else ()),
                                     scale=cur[:, 2, t, 2 * k + r:2 * k + r + 1])
                    next_slot(2)
                    if pair == 0:
                        take_job(J_GZ, SZ[:, :, :], ACT.Silu)
                    next_slot(3)
                    for e in range(2):
                        k = 2 * pair + e
                        wait("t1_turned", k + 1)
                        activate(flat(X[e]["TT"]), bank[2 + e][:, :], ACT.Copy, "tt1_made", k + 1)
                    next_slot()
                    for l in range(LEVELS):
                        for e in range(2):
                            n = pair * 2 * LEVELS + 2 * l + e + 1
                            wait("v_done", n)
                            activate(flat(X[e]["V"]), bank[e][:, :], ACT.Copy, "v_made", n)
                        next_slot()
                        next_slot()
                    for e in range(2):
                        k = 2 * pair + e
                        wait("wt_done", k + 1)
                        activate(flat(X[e]["WT"]), bank[e][:, :], ACT.Copy, "wt_made", k + 1)
                    next_slot(3)
                    for j in range(NCK):
                        t, h = divmod(j, 2)
                        rows_ = slice(CH * h, CH * h + CH)
                        for e in range(2):
                            k = 2 * pair + e
                            n = pair * 2 * NCK + 2 * j + e + 1
                            wait("qs_done", n)
                            if j:
                                wait("o_made", n - 2)
                            for r in range(2):
                                activate(X[e]["O1"][rows_, r * DV:(r + 1) * DV],
                                         bank[2 + e][rows_, P + r * DV:P + (r + 1) * DV],
                                         ACT.Copy, *(("o1_made", n) if r else ()),
                                         scale=cur[rows_, 1, t, 2 * k + r:2 * k + r + 1])
                        next_slot()
                        next_slot()

                delta_pair(0)
                for n, job in enumerate((J_FQ, J_FK)):
                    if n:
                        wait("f_turned", n)
                        for h in range(2):
                            activate(FQ[:, 2 * h:2 * h + 2, :].rearrange("p a b -> p (a b)"), bank[h][:, :], ACT.Copy,
                                     *(("f_made", 1) if h else ()))
                    take_job(job, stage[:, :, :])
                    next_slot()
                    next_slot()
                delta_pair(1)
                take_job(J_FV, FV)
                fence(act, "act", i, 4, o, lambda: next_slot(2))
                take_job(J_CC, stage[:, :, :])
                next_slot(2)
                wait("rms_in", 1)
                activate(rms[:, :], rms[:, :], ACT.Ln, bias=eps_b[:, 0:1], scale=1.0 / DV)
                o.after()
                activate(rms[:, :], rms[:, :], ACT.Exp, "rms_out", 1, scale=-0.5)
                next_slot(7)
                wait("fmax_made", 1)
                for f in range(KPC):
                    for t in range(MT):
                        s_ = SC[:, f, t * P:(1 + 2 * t) * P]
                        activate(s_, s_, ACT.Exp, bias=fmax[:, 0, MT * f + t:MT * f + t + 1],
                                 accum_out=fmax[:, 1, MT * f + t:MT * f + t + 1])
                o.after()
                act.sem_inc(N["fexp_made"].sem, 1)
                next_slot()
                wait("yb_turned", 1)
                for h in range(2):
                    activate(yT[1][:, bass.ds(i * BPC + 2 * h, 2), :],
                             bank[h][:, :].rearrange("p (a b) -> p a b", a=2), ACT.Copy,
                             *(("yb_made", 1) if h else ()))
                wait("finv_made", 1)
                for f in range(KPC):
                    for t in range(MT):
                        s_ = SC[:, f, t * P:(1 + 2 * t) * P]
                        activate(s_, s_, ACT.Copy, *(("prob_made", 1) if (f, t) == (KPC - 1, MT - 1) else ()),
                                 scale=fmax[:, 1, MT * f + t:MT * f + t + 1])
                next_slot(2)
                next_slot()
                wait("prob_turned", 1)
                for f in range(KPC):
                    activate(PT[:, f, :], bank[f][:, 0:3 * P], ACT.Copy, *(("probT_made", 1) if f == KPC - 1 else ()))
                next_slot(4)
                for n, job in ((1, J_CH), (2, J_CB)):
                    wait("c_turned", n)
                    if n == 1:
                        for h in range(2):
                            activate(FQ[:, 2 * h:2 * h + 2, :].rearrange("p a b -> p (a b)"), bank[h][:, :], ACT.Copy,
                                     *(("cc_made", 1) if h else ()))
                    take_job(job, stage[:, :, :])
                    next_slot(2)
                assert count[0] >= 2 * MAIN_UNITS
                o.end(NCH)
            meet(act, "act", 1, o)

            def hi_split(dst, src, name, first):
                for n in range(4):
                    activate(dst[:, 4 * n:4 * n + 4, :], src[:, 4 * n:4 * n + 4, :], ACT.Copy, name, first + n)

            for b in range(3):
                o.begin(0, 10)
                if b:
                    job_wait(act, J_MERGE + 2 * NCH * b - 1)
                hi_split(z_hi, yT[b], "y_hi", 4 * b + 1)
                o.end()
                with act.Fori(0, NCH) as i:
                    o.begin(i, 10)
                    count = [0]
                    next_slot = slots(i, 2 * UPJ, J_MERGE * UPJ + b * 2 * UPJ * NCH, 2 * UPJ,
                                      R_MERGE + b * 2 * UPJ * NCH, plain_place, count)
                    for _ in range(KT + 1):
                        next_slot()
                    j = J_MERGE + 2 * NCH * b
                    job_wait(act, i * 2 + j)
                    act.wait_ge(acc_free[1].sem, i + (j // 2 + 1))
                    o.do_count(a.activation(sig[:, :, :], acc[0][:, :, :], ACT.Sigmoid),
                               acc_free[0].sem, i + (j // 2 + 2))
                    while count[0] < 4 * UPJ:
                        next_slot()
                    o.end(NCH)
            act.wait_ge(N["y_lo"].sem, 3 * 4)
            act.dma_start(x1[:, :, :], x[0].rearrange("(m p) n -> p m n", p=P)).then_inc(ln_in.sem, 16)
            act.dma_start(ln_g[:, :], ln1_g[0].partition_broadcast(P)).then_inc(ln_in.sem, 16)
            o.begin(0, 40)
            for n in range(8):
                act.wait_ge(N["z_turned"].sem, n + 1)
                activate(z_hi[:, 2 * n:2 * n + 2, :], bank[n % 4][:, :].rearrange("p (a b) -> p a b", a=2), ACT.Copy, "z_hi_made", n + 1)

            act.wait_ge(N["merged_made"].sem, 3 * NCH)
            act.dma_start(ln_b[:, :], ln1_b[0].partition_broadcast(P)).then_inc(ln_in.sem, 16)

            def gate_rows(which, dst):
                for n in range(NCH):
                    act.wait_ge(N["gate_done"].sem, which * NCH + n + 1)
                    activate(dst[:, n * NC:(n + 1) * NC], bank[n][:, :], ACT.Copy, "gate_made", which * NCH + n + 1)

            gate_rows(0, gate_b)
            o.end()
            with act.Fori(0, NCH // 2) as i:
                count = [0]
                next_slot = slots(i, 2 * UPJ, J_OUT * UPJ, 2 * UPJ, R_OUT, plain_place, count)
                while count[0] < 4 * UPJ:
                    next_slot()

            def ln_scale(which):
                act.wait_ge(N["ln_var"].sem, (which + 1) * MT)
                activate(rstd[:, :], aggr[:, :, 1], ACT.Ln, bias=eps_b[:, 2:3])
                o.after()
                activate(rstd[:, :], rstd[:, :], ACT.Exp, "ln_rstd", which + 1, scale=-0.5)

            o.begin(0, 60)
            gate_rows(1, gate2_b)
            ln_scale(0)
            def make_hi(g):
                act.wait_ge(N["u2_even"].sem, g + 1)
                act.wait_ge(N["u2_odd"].sem, g + 1)
                activate(u_hi[:, 2 * g:2 * g + 2, :], u2(g, 2), ACT.Copy, "u2_hi", g + 1)

            for g in range(KT // 2):
                k = 2 * g
                act.wait_ge(N["xhat_turned"].sem, k + 1)
                if g >= 2:
                    act.wait_ge(N["u2_lo"].sem, g - 1)
                activate(u2(g, 0), bank[k % 4][:, 0:S], ACT.Identity, "u2_even", g + 1,
                         scale=lnc[:, 0, k:k + 1], bias=lnc[:, 1, k:k + 1])
                if g:
                    make_hi(g - 1)
            make_hi(KT // 2 - 1)
            o.end()
            act.wait_ge(N["u2_lo"].sem, KT // 2)
            with act.Fori(0, FFQ) as i:
                o.begin(i, 60)
                count = [0]
                next_slot = slots(i, FF_JOBS * UPJ, J_FF * UPJ, FF_JOBS * UPJ, R_FF, plain_place, count)
                for j in range(NCH):
                    while count[0] < (j + 1) * KT:
                        next_slot()
                    job_wait(act, i * FF_JOBS + (J_FF + j))
                    if j:
                        act.wait_ge(N["h_turned"].sem, N["h_turned"].value(i, j))
                    o.do_count(a.activation(stage[:, :, :], acc[j % 2][:, :, :], ACT.Relu),
                               acc_free[j % 2].sem, i * (FF_JOBS // 2) + ((J_FF + j) // 2 + 2))
                    o.after()
                    activate(stage[:, :, :], stage[:, :, :], ACT.Square, "squared", j + 1)
                    next_slot(3)
                    act.wait_ge(N["h_turned"].sem, N["h_turned"].value(i, j + 1))
                    for h in range(2):
                        activate(z_hi[:, 4 * j + 2 * h:4 * j + 2 * h + 2, :],
                                 bank[2 * (j % 2) + h][:, :].rearrange("p (a b) -> p a b", a=2), ACT.Copy,
                                 *(("h_hi", j + 1) if h else ()))
                while count[0] < FF_JOBS * KT:
                    next_slot()
                o.end(FFQ)
            act.wait_ge(N["base_made"].sem, 1)
            act.dma_start(ln_g[:, :], ln2_g[0].partition_broadcast(P)).then_inc(ln_in.sem, 16)
            act.dma_start(ln_b[:, :], ln2_b[0].partition_broadcast(P)).then_inc(ln_in.sem, 16)
            o.begin(0, 20)
            ln_scale(1)
            o.end()

        @block.vector
        def _(dve):
            o = Order(dve, own["dve"])
            v = nc.vector

            def tt(dst, in0, in1, op, name=None, k=None):
                o.do(v.tensor_tensor(dst, in0, in1, op), N[name] if name else None, k)

            def ts(dst, in0, s1, s2, op0, op1=ALU.bypass, name=None, k=None):
                o.do(v.tensor_scalar(dst, in0, s1, s2, op0, op1), N[name] if name else None, k)

            def stt(dst, in0, scalar, in1, op0, op1, name=None, k=None):
                o.do(v.scalar_tensor_tensor(dst, in0, scalar, in1, op0, op1), N[name] if name else None, k)

            def copy(dst, src, name=None, k=None):
                o.do(v.tensor_copy(dst, src), N[name] if name else None, k)

            def lo_unit(n, u, rl):
                dve.wait_ge(hi_ready.sem, n + 1)
                dve.wait_ge(units_used.sem, n + 1)
                v.tensor_tensor(w_lo[:, u % PARTS, :, :], raw[:, rl % RAWS, :, :], w_hi[:, u % PARTS, :, :],
                                ALU.subtract).then_inc(lo_ready.sem, 1)
                dve.wait_ge(lo_ready.sem, n + 1)
                dve.sem_inc(raw_free.sem, 1)

            def mod_unit(m, r, rl, into):
                dve.wait_ge(raw_ready[rl % RAWS].sem, r)
                for q in range(UK):
                    k = UK * m + q
                    src = raw[:, rl % RAWS, q, :]
                    o.after()
                    if k == 0:
                        ts(into, src, c_act[:, 0:1], None, ALU.mult)
                    else:
                        stt(into, src, c_act[:, k:k + 1], into, ALU.mult, ALU.add)
                o.after()
                dve.sem_inc(raw_free.sem, 1)

            def slots(i, units, unit0, raws, raw0, place, count):
                def one():
                    s = count[0]
                    count[0] += 1
                    if s % 2 and s // 2 < units:
                        u = s // 2 + LEAD
                        rl = place(u)
                        lo_unit(i * units + (unit0 + u), u, rl)
                        m = mod_after(u) if place is raw_place and u < MAIN_UNITS else None
                        if m is not None:
                            n = m // UPJ
                            if m % UPJ == 0 and n >= 2:
                                dve.wait_ge(N["mcol_done"].sem, N["mcol_done"].value(i, n - 1))
                            rl += 1
                            mod_unit(m % UPJ, i * (16 * raws // RAWS) + 16 * ((raw0 + rl) // RAWS + 1), rl, macc[:, n % 2, :])
                            if m % UPJ == UPJ - 1:
                                dve.sem_inc(N["macc_ready"].sem, 1)

                def go_on(times=1):
                    for _ in range(times):
                        one()
                return go_on

            dve.sem_inc(raw_free.sem, RAWS)
            with dve.Fori(0, NMOD_FIRST // 2) as i:
                o.begin(i, 40)
                dve.wait_ge(N["c_made"].sem, 1)
                for h in range(2):
                    dve.wait_ge(N["mcol_first"].sem, 2 * i + (h + 1))
                    for m in range(UPJ):
                        rl = h * UPJ + m
                        mod_unit(m, i * (16 * 2 * UPJ // RAWS) + 16 * (rl // RAWS + 1), rl, macc[:, h, :])
                    dve.sem_inc(N["macc_first"].sem, 1)
                o.end(NMOD_FIRST // 2)
            o.begin(0, 40)
            dve.wait_ge(N["mcol_first"].sem, NMOD_FIRST + 2)
            dve.wait_ge(N["rows_in"].sem, 1)
            tt(mod[:, 0:2 * KT], bank[1][:, KT:3 * KT], bada[:, 0:2 * KT], ALU.add)
            o.after()
            ts(mod[:, KT:2 * KT], mod[:, KT:2 * KT], 1.0, None, ALU.add, name="mod_first", k=1)
            dve.wait_ge(N["x_copied"].sem, 8)
            o.after()

            def make_lo(g):
                dve.wait_ge(N["u_hi_made"].sem, g + 1)
                tt(u_lo[:, 2 * g:2 * g + 2, :], uT[:, 2 * g:2 * g + 2, :], u_hi[:, 2 * g:2 * g + 2, :], ALU.subtract, "u_lo_made", g + 1)

            for g in range(KT // 2):
                k = 2 * g + 1
                ts(uT[:, k, :], uT[:, k, :], mod[:, KT + k:KT + k + 1], mod[:, k:k + 1], ALU.mult, ALU.add, name="u_odd", k=g + 1)
                if g >= 2:
                    make_lo(g - 2)
            make_lo(KT // 2 - 2)
            make_lo(KT // 2 - 1)
            for u in range(LEAD):
                lo_unit(u, u, u)
            dve.wait_ge(N["small_in"].sem, 1)
            dve.wait_ge(g_in.sem, 16 * 4)

            def both(t):
                return t.unsqueeze(1).broadcast_to([P, MT, t.shape[1]])

            ts(sm2[:, :, 0:VH], sm[:, :, 0:VH], -1.0, None, ALU.mult)
            tt(sm2[:, :, VH:2 * VH], sm[:, :, VH:2 * VH], both(gpar[:, VH:2 * VH]), ALU.add)
            stt(sm2[:, :, 2 * VH:NSM], sm[:, :, 2 * VH:NSM], -1.0, both(gpar[:, 2 * VH:2 * VH + FH]), ALU.mult, ALU.subtract)
            o.after()
            ts(flat(sm), flat(sm2), -1.0, None, ALU.mult)
            o.after()
            tt(flat(sm), flat(sm), flat(sm2), ALU.min, "small_neg", 1)
            dve.wait_ge(N["small_exp"].sem, 1)
            ts(flat(log_s), flat(sm), 2.0, None, ALU.add)
            o.after()
            o.do(v.reciprocal(flat(log_s), flat(log_s)))
            o.after()
            tt(flat(log_s), flat(log_s), flat(sm), ALU.mult)
            o.after()
            tt(flat(log_s2), flat(log_s), flat(log_s), ALU.mult)
            o.after()
            ts(flat(sm), flat(log_s2), 1.0 / (2 * LOG_TERMS + 1), None, ALU.mult)
            for n in range(LOG_TERMS - 1, 0, -1):
                o.after()
                stt(flat(sm), flat(sm), 1.0 / (2 * n + 1), flat(log_s2), ALU.add, ALU.mult)
            o.after()
            stt(flat(sm), flat(sm), 1.0, flat(log_s), ALU.add, ALU.mult)
            o.after()
            ts(flat(sm), flat(sm), 2.0, None, ALU.mult)
            o.after()
            stt(flat(sm2), flat(sm2), 0.0, flat(sm), ALU.max, ALU.add, "small_sp", 1)
            o.after()
            stt(sm2[:, :, VH:2 * VH], sm2[:, :, VH:2 * VH], -1.0, both(gpar[:, 0:VH]), ALU.mult, ALU.mult)
            ts(sm2[:, :, 2 * VH:NSM], sm2[:, :, 2 * VH:NSM], -1.0, None, ALU.mult)
            o.after()
            dve.sem_inc(N["logs_made"].sem, 1)
            dve.wait_ge(N["sums_in"].sem, 1)
            tt(heads[:, 3, :, :], heads[:, 2, :, :], heads[:, 1, :, :], ALU.mult)
            tt(heads[:, 4, :, :], bank[1][:, MT * VH:2 * MT * VH].rearrange("p (m h) -> p m h", m=MT), heads[:, 0, :, :],
               ALU.subtract, "decay_left", 1)
            o.end()

            with dve.Fori(0, NCH) as i:
                o.begin(i, 400)
                count = [0]
                next_slot = slots(i, MAIN_UNITS, 0, MAIN_RAW, R_MAIN, raw_place, count)

                def wait(name, k):
                    dve.wait_ge(N[name].sem, N[name].value(i, k))

                def until(job):
                    while count[0] < (job + 1) * KT:
                        next_slot()

                def taps(dst, srcs, w, ntap, sig_name, sig_k, between=0, first=0):
                    for n in range(first, ntap):
                        o.after()
                        for b in range(BPC):
                            tap = ntap - 1 - n
                            last = n == ntap - 1 and b == BPC - 1
                            args = (sig_name, sig_k) if last else (None, None)
                            if n == 0:
                                ts(dst[:, b, :], srcs(b), w(b, tap), None, ALU.mult, name=args[0], k=args[1])
                            else:
                                stt(dst[:, b, n:S], srcs(b)[:, 0:S - n], w(b, tap), dst[:, b, n:S], ALU.mult, ALU.add, *args)
                        next_slot(between)

                def mod_columns(n):
                    wait("mcol_done", n + 1)
                    at = i * (MODS * BPC) + (NMOD_FIRST + n) * BPC
                    tt(mod[:, bass.ds(at, BPC)], bank[MOD_BANK[n]][:, 0:BPC], bada[:, bass.ds(at, BPC)], ALU.add, "mod_made", n + 1)

                def halves(n):
                    return lambda b: bank[n + b // 2][:, (b % 2) * S:(b % 2 + 1) * S]

                fence(dve, "dve", i, 1, o)
                copy(cur[:, :, :, :].rearrange("p a m h -> p (a m) h"),
                     heads[:, :, :, :].rearrange("p a m h -> p (a m) h")[:, :, bass.ds(i * VPC, VPC)])
                copy(cur_cd[:, :, :], cd[:, :, bass.ds(i * VPC, VPC)])
                copy(cur_f[:, :, :], fcum[:, :, bass.ds(i * KPC, KPC)])
                for s in range(3):
                    copy(cur_cwg[:, s, :, :], cwg[:, :, bass.ds(i * BPC + s * KT, BPC)])
                copy(cur_cwa[:, :, :], cwa[:, :, bass.ds(i * BPC, BPC)])
                o.after()
                dve.sem_inc(N["cur_made"].sem, 1)
                for k, job in enumerate((J_GQ, J_GK, J_GV)):
                    until(job)
                    next_slot(4)
                    wait("tap_made", k + 1)
                    taps((QC, KC, VC)[k], halves(2 * (k % 2)), lambda b, tap: cur_cwg[:, k, tap, b:b + 1], TAPS_G, "conv_made", k + 1, 1, 1)
                    if k == 1:
                        next_slot(9)
                        wait("rn_made", 1)
                        for n in range(4):
                            src = (QC, KC)[n // 2][:, 2 * (n % 2):2 * (n % 2) + 2, :].rearrange("p a b -> p (a b)")
                            tt(src, src, norm_tmp[n], ALU.mult, *(("qk_made", 1) if n == 3 else ()))
                next_slot(5)
                next_slot(2)
                mod_columns(0)
                next_slot()

                def delta_pair(pair):
                    fence(dve, "dve", i, 2 + pair, o, next_slot)
                    for e in range(2):
                        k = 2 * pair + e
                        wait("gb_done", k + 1)
                        for q in range(4):
                            t, r = divmod(q, 2)
                            ts(X[e]["V"][:, q, :], bank[2 + e][:, q * P:(q + 1) * P], cur[:, 0, t, 2 * k + r:2 * k + r + 1],
                               0.0, ALU.subtract, ALU.min, *(("d_made", k + 1) if q == 3 else ()))
                    for e in range(2):
                        k = 2 * pair + e
                        wait("kk_done", k + 1)
                        wait("decay_made", k + 1)

                        def over_heads(lo):
                            a = bank[e][:, lo:lo + MT * P].rearrange("p (t c) -> p t c", t=MT)
                            return a.unsqueeze(2).broadcast_to([P, MT, 2, P])

                        four = lambda t: t[:, :, :].rearrange("p (t r) c -> p t r c", r=2)
                        tt(four(X[e]["KB"]), over_heads(0), four(X[e]["V"]), ALU.mult, "low_made", k + 1)
                        tt(four(X[e]["IT"]), over_heads(MT * P), four(X[e]["V"]), ALU.mult, "it_made", k + 1)
                    next_slot(4)
                    for e in range(2):
                        k = 2 * pair + e
                        wait("b_made", pair * 2 * (LEVELS + 1) + e + 1)
                        tt(X[e]["T"][:, :, :], ident[:, :].unsqueeze(1).broadcast_to([P, 4, P]), X[e]["B"][:, :, :],
                           ALU.subtract, "t1_made", k + 1)
                    next_slot(4)
                    for l in range(LEVELS):
                        next_slot()
                        for e in range(2):
                            k = 2 * pair + e
                            n = pair * 2 * LEVELS + 2 * l + e + 1
                            wait("d_done", n)
                            if l == 0:
                                wait("tt1_made", k + 1)
                            dst = halves_of(X[e]["TT"], l, 1)
                            tt(dst, dst, d_halves(e, 0, l), ALU.subtract, "tt_made", n)
                            if l < LEVELS - 1:
                                n = pair * 2 * (LEVELS - 1) + 2 * l + e + 1
                                dst = halves_of(X[e]["T"], l, 0)
                                tt(dst, dst, d_halves(e, 1, l), ALU.subtract, "t_made", n)
                        next_slot()
                    for e in range(2):
                        k = 2 * pair + e
                        wait("u_done", k + 1)
                        copy(X[e]["UU"], bank[2 + e][:, 0:4 * DV].rearrange("p (a b) -> p a b", a=4), "uu_made", k + 1)
                    o.after()
                    next_slot(3)
                    for j in range(NCK):
                        t, h = divmod(j, 2)
                        rw = slice(CH * h, CH * h + CH)
                        first = pair * 2 * NCK + 2 * j + 1
                        for e in range(2):
                            x_ = X[e]
                            wait("ws_done", first + e)
                            tt(x_["VN"][rw, :], x_["UU"][rw, 2 * t:2 * t + 2, :].rearrange("p a b -> p (a b)"),
                               bank[e][rw, 0:P], ALU.subtract)
                        o.after()
                        for e in range(2):
                            k = 2 * pair + e
                            x_ = X[e]
                            tt(x_["VS"][rw, :].rearrange("p (a b) -> p a b", a=2), x_["VN"][rw, :].rearrange("p (a b) -> p a b", a=2),
                               cur[rw, 4, t, 2 * k:2 * k + 2].unsqueeze(2).broadcast_to([CH, 2, DV]), ALU.mult, "vs_made", first + e)
                        next_slot()
                        for e in range(2):
                            k = 2 * pair + e
                            x_ = X[e]
                            wait("su_done", first + e)
                            for r in range(2):
                                st = x_["ST"][:, r * DV:(r + 1) * DV]
                                stt(st, st, cur_cd[:, j, 2 * k + r:2 * k + r + 1], bank[2 + e][:, 2 * P + r * DV:2 * P + (r + 1) * DV],
                                    ALU.mult, ALU.add, *(("s_made", first + e) if r else ()))
                        for e in range(2):
                            k = 2 * pair + e
                            wait("in_done", first + e)
                            wait("o1_made", first + e)
                            tt(vtok[rw, t, k * P:(k + 1) * P], X[e]["O1"][rw, :], bank[e][rw, P:2 * P], ALU.add, "o_made", first + e)
                        next_slot()

                delta_pair(0)
                for n, job in enumerate((J_FQ, J_FK)):
                    until(job)
                    next_slot()
                    if n == 1:
                        wait("f_turned", 2)
                        for h in range(2):
                            copy(FK[:, 2 * h:2 * h + 2, :].rearrange("p a b -> p (a b)"), bank[2 + h][:, :], *(("f_made", 2) if h else ()))
                        mod_columns(1)
                    next_slot()
                delta_pair(1)
                fence(dve, "dve", i, 4, o, lambda: next_slot(2))
                for m in range(MT):
                    wait("osq_made", m + 1)
                    o.do(v.tensor_reduce(rms[:, m * VPC:(m + 1) * VPC], flat(osq[m]).rearrange("p (h d) -> p h d", d=DV),
                                         mybir.AxisListType.X, ALU.add), *((N["rms_in"], 1) if m else ()))
                wait("cum_done", 1)
                for f in range(KPC):
                    ck = bank[2 + f // 2][:, (f % 2) * S:(f % 2 + 1) * S]
                    stt(BI[:, f, 0:P], ck[:, 0:P], cur_f[:, 0, f:f + 1], causal_big[:, :], ALU.subtract, ALU.add)
                    ts(BI[:, f, P:2 * P], ck[:, 0:P], cur_f[:, 1, f:f + 1], None, ALU.subtract)
                    stt(BI[:, f, 2 * P:3 * P], ck[:, P:2 * P], cur_f[:, 1, f:f + 1], causal_big[:, :], ALU.subtract, ALU.add,
                        *(("bias_made", 1) if f == KPC - 1 else ()))
                next_slot(2)
                wait("rms_out", 1)
                for m in range(MT):
                    o3 = vtok[:, m, :].rearrange("p (h d) -> p h d", d=DV)
                    tt(o3, o3, rms[:, m * VPC:(m + 1) * VPC].unsqueeze(2).broadcast_to([P, VPC, DV]), ALU.mult, *(("rms_used", 1) if m else ()))
                next_slot(2)
                wait("scores_done", 1)
                for f in range(KPC):
                    stt(SC[:, f, :], bank[f][:, 0:3 * P], float(P) ** -0.5, BI[:, f, :], ALU.mult, ALU.subtract,
                        *(("scored", 1) if f == KPC - 1 else ()))
                next_slot(2)
                o.after()
                for f in range(KPC):
                    for t in range(MT):
                        o.do(v.tensor_reduce(fmax[:, 0, MT * f + t:MT * f + t + 1], SC[:, f, t * P:(1 + 2 * t) * P],
                                             mybir.AxisListType.X, ALU.max, negate=True),
                             *((N["fmax_made"], 1) if (f, t) == (KPC - 1, MT - 1) else ()))
                next_slot(4)
                mod_columns(2)
                wait("fexp_made", 1)
                o.do(v.reciprocal(fmax[:, 1, :], fmax[:, 1, :]), N["finv_made"], 1)
                next_slot(6)
                wait("yc_done", 1)
                for h in range(2):
                    for q in range(2):
                        copy(yT[2][:, bass.ds(i * BPC + 2 * h + q, 1), :].rearrange("p a b -> p (a b)"), bank[2 * h + q][:, 0:S],
                             *(("yc_made", 1) if (h, q) == (1, 1) else ()))
                next_slot()
                mod_columns(3)
                until(J_CH)
                next_slot()
                wait("cc_made", 1)
                wait("c_turned", 2)
                o.after()
                for h in range(2):
                    c2 = FQ[:, 2 * h:2 * h + 2, :].rearrange("p a b -> p (a b)")
                    tt(c2, c2, bank[2 + h][:, :], ALU.mult, *(("ch_made", 1) if h else ()))
                taps(FK, lambda b: FQ[:, b, :], lambda b, tap: cur_cwa[:, tap, b:b + 1], TAPS_A, "conv3_made", 1)
                next_slot()
                until(J_CB)
                next_slot()
                wait("c_turned", 3)
                for h in range(2):
                    tt(yT[0][:, bass.ds(i * BPC + 2 * h, 2), :].rearrange("p a b -> p (a b)"),
                       FK[:, 2 * h:2 * h + 2, :].rearrange("p a b -> p (a b)"), bank[h][:, :], ALU.mult, *(("ya_made", 1) if h else ()))
                next_slot()
                assert count[0] >= 2 * MAIN_UNITS
                o.end(NCH)
            o.begin(0, 8)
            scale2 = mod[:, 4 * KT:5 * KT]
            ts(scale2, scale2, 1.0, None, ALU.add)
            o.after()
            tt(lnc[:, :, :], lnc[:, :, :], scale2.unsqueeze(1).broadcast_to([P, 2, KT]), ALU.mult)
            o.after()
            tt(lnc[:, 1, :], lnc[:, 1, :], mod[:, 3 * KT:4 * KT], ALU.add)
            o.end()
            meet(dve, "dve", 1, o)

            for b in range(3):
                for n in range(4):
                    dve.wait_ge(N["y_hi"].sem, 4 * b + n + 1)
                    tt(z_lo[:, 4 * n:4 * n + 4, :], yT[b][:, 4 * n:4 * n + 4, :], z_hi[:, 4 * n:4 * n + 4, :], ALU.subtract, "y_lo", 4 * b + n + 1)
                with dve.Fori(0, NCH) as i:
                    o.begin(i, 4)
                    count = [0]
                    next_slot = slots(i, 2 * UPJ, J_MERGE * UPJ + b * 2 * UPJ * NCH, 2 * UPJ,
                                      R_MERGE + b * 2 * UPJ * NCH, plain_place, count)
                    for _ in range(4 * UPJ):
                        next_slot()
                    j = J_MERGE + 2 * NCH * b
                    job_wait(dve, i * 2 + (j + 1))
                    dve.wait_ge(acc_free[0].sem, i + (j // 2 + 2))
                    mg = merged[:, :, bass.ds(i * NC, NC)]
                    if b:
                        o.do_count(v.tensor_tensor(gated[:, :, :], sig[:, :, :], acc[1][:, :, :], ALU.mult), acc_free[1].sem, i + (j // 2 + 2))
                        o.after()
                        o.do_count(v.tensor_tensor(mg, mg, gated[:, :, :], ALU.add), N["merged_made"].sem, i + (b * NCH + 1))
                    else:
                        o.do_count(v.tensor_tensor(mg, sig[:, :, :], acc[1][:, :, :], ALU.mult), acc_free[1].sem, i + (j // 2 + 2))
                        o.after()
                        dve.sem_inc(N["merged_made"].sem, 1)
                    o.end(NCH)
            for n in range(8):
                dve.wait_ge(N["z_hi_made"].sem, n + 1)
                tt(z_lo[:, 2 * n:2 * n + 2, :].rearrange("p a b -> p (a b)"), bank[n % 4][:, :],
                   z_hi[:, 2 * n:2 * n + 2, :].rearrange("p a b -> p (a b)"), ALU.subtract, "z_lo_made", n + 1)
            dve.wait_ge(ln_in.sem, 16 * 3)
            o.begin(0, 4)
            ts(ln_g[:, :], ln_g[:, :], ALPHA, None, ALU.mult)
            ts(ln_b[:, :], ln_b[:, :], ALPHA, None, ALU.mult, name="ln_scaled", k=1)
            o.end()
            dve.wait_ge(N["gate_made"].sem, NCH)
            with dve.Fori(0, NCH // 2) as i:
                o.begin(i, 8)
                count = [0]
                next_slot = slots(i, 2 * UPJ, J_OUT * UPJ, 2 * UPJ, R_OUT, plain_place, count)
                for j in range(2):
                    while count[0] < (j + 1) * KT:
                        next_slot()
                    job_wait(dve, i * 2 + (J_OUT + j))
                    cols = bass.ds(i * (2 * NC) + j * NC, NC)
                    gb = gate_b[:, cols].unsqueeze(1).broadcast_to([P, MT, NC])
                    o.do_count(v.tensor_tensor(xr[:, :, cols], acc[j][:, :, :], gb, ALU.mult), acc_free[j].sem, i + (J_OUT // 2 + 2))
                    o.after()
                    stt(xr[:, :, cols], x1[:, :, cols], ALPHA, xr[:, :, cols], ALU.mult, ALU.add)
                    o.after()
                    for m in range(MT):
                        o.do(v.bn_stats(stats[:, m, bass.ds(i * 2 + j, 1), :].rearrange("p a b -> p (a b)"), xr[:, m, cols]))
                    o.after()
                o.end(NCH // 2)
            o.begin(0, 60)

            def ln_statistics(which):
                for m in range(MT):
                    o.do(v.bn_aggr(aggr[:, m, :], stats[:, m, :, :].rearrange("p a b -> p (a b)")), N["ln_var"], which * MT + m + 1)
                dve.wait_ge(N["ln_rstd"].sem, which + 1)

            ln_statistics(0)
            for n in range(NCH):
                for m in range(MT):
                    ts(x1[:, m, n * NC:(n + 1) * NC], xr[:, m, n * NC:(n + 1) * NC], aggr[:, m, 0:1], rstd[:, m:m + 1],
                       ALU.subtract, ALU.mult, *(("xhat_made", n + 1) if m else ()))

            def make_lo(g):
                dve.wait_ge(N["u2_hi"].sem, g + 1)
                tt(u_lo[:, 2 * g:2 * g + 2, :], u2(g, 2), u_hi[:, 2 * g:2 * g + 2, :], ALU.subtract, "u2_lo", g + 1)

            for g in range(KT // 2):
                k = 2 * g + 1
                dve.wait_ge(N["xhat_turned"].sem, k + 1)
                if g >= 2:
                    dve.wait_ge(N["u2_lo"].sem, g - 1)
                ts(u2(g, 1), bank[k % 4][:, 0:S], lnc[:, 0, k:k + 1], lnc[:, 1, k:k + 1], ALU.mult, ALU.add, name="u2_odd", k=g + 1)
                if g:
                    make_lo(g - 1)
            make_lo(KT // 2 - 1)
            o.end()
            with dve.Fori(0, FFQ) as i:
                o.begin(i, 20)
                count = [0]
                next_slot = slots(i, FF_JOBS * UPJ, J_FF * UPJ, FF_JOBS * UPJ, R_FF, plain_place, count)
                for j in range(NCH):
                    while count[0] < (j + 1) * KT:
                        next_slot()
                    next_slot()
                    next_slot()
                    dve.wait_ge(N["h_hi"].sem, N["h_hi"].value(i, j + 1))
                    for h in range(2):
                        tt(z_lo[:, 4 * j + 2 * h:4 * j + 2 * h + 2, :].rearrange("p a b -> p (a b)"), bank[2 * (j % 2) + h][:, :],
                           z_hi[:, 4 * j + 2 * h:4 * j + 2 * h + 2, :].rearrange("p a b -> p (a b)"), ALU.subtract, "h_lo", 2 * j + h + 1)
                for j in range(NCH, FF_JOBS):
                    while count[0] < (j + 1) * KT:
                        next_slot()
                    job_wait(dve, i * FF_JOBS + (J_FF + j))
                    cols = slice((j - NCH) * NC, (j - NCH + 1) * NC)
                    gb = gate2_b[:, cols].unsqueeze(1).broadcast_to([P, MT, NC])
                    o.after()
                    o.do_count(v.tensor_tensor(ff_part[:, :, :], acc[j % 2][:, :, :], gb, ALU.mult), acc_free[j % 2].sem,
                               i * (FF_JOBS // 2) + ((J_FF + j) // 2 + 2))
                    dve.wait_ge(N["base_made"].sem, 1)
                    o.after()
                    tt(xr[:, :, cols], xr[:, :, cols], ff_part[:, :, :], ALU.add)
                    o.after()
                    for m in range(MT):
                        o.do(v.bn_stats(stats[:, m, j - NCH, :], xr[:, m, cols]))
                o.end(FFQ)
            o.begin(0, 60)
            ln_statistics(1)
            dve.wait_ge(ln_in.sem, 16 * 5)
            for m in range(MT):
                stt(xr[:, m, :], xr[:, m, :], aggr[:, m, 0:1], ln_g[:, :], ALU.subtract, ALU.mult)
                o.after()
                stt(x1[:, m, :], xr[:, m, :], rstd[:, m:m + 1], ln_b[:, :], ALU.mult, ALU.add, "out_made", m + 1)
            o.after()

        @block.tensor
        def _(pe):
            t_ = nc.tensor

            def mm(dst, lhsT, rhs, start=True, stop=True):
                return t_.matmul(dst, lhsT, rhs, start=start, stop=stop)

            def turn(dst, src):
                return t_.transpose(dst, src, ident[:, :])

            def k_tile(n, u, q, dst, j, left):
                k = UK * (u % UPJ) + q
                hi, lo = left
                if q == 0:
                    pe.wait_ge(lo_ready.sem, n + 1)
                if k == 0:
                    pe.wait_ge(acc_free[dst].sem, j)
                sl = u % PARTS
                for m in range(MT):
                    ms = slice(m * P, (m + 1) * P)
                    mm(acc[dst][:, m, :], hi[:, k, ms], w_hi[:, sl, q, :], k == 0, False)
                    mm(acc[dst][:, m, :], hi[:, k, ms], w_lo[:, sl, q, :], False, False)
                    last = mm(acc[dst][:, m, :], lo[:, k, ms], w_hi[:, sl, q, :], False, k == KT - 1)
                if q == UK - 1:
                    last.then_inc(units_used.sem, 1)

            def slots(i, units, unit0, count, left):
                def one():
                    s = count[0]
                    count[0] += 1
                    if s < 2 * units:
                        job = s // KT
                        k_tile(i * units + (unit0 + s // 2), s // 2, s % 2, job % 2,
                               i * (units // UPJ // 2) + (unit0 // UPJ + job) // 2 + 1, left(job, s))

                def go_on(times=1):
                    for _ in range(times):
                        one()
                return go_on

            pe.sem_inc(units_used.sem, PARTS)
            pe.sem_inc(acc_free[0].sem, 1)
            pe.sem_inc(acc_free[1].sem, 1)
            pe.sem_inc(N["mcol_first"].sem, 2)
            pe.wait_ge(c_in.sem, 16)
            pe.wait_ge(N["ident_made"].sem, 1)
            t_.transpose(bank[1][:, 0:KT], rows[0:KT, 4, :], ident[0:KT, 0:KT]).then_inc(N["c_turned_in"].sem, 1)
            pe.wait_ge(x_in.sem, 16)
            for n in range(8):
                if n >= 2:
                    pe.wait_ge(N["x_copied"].sem, n - 1)
                for q in range(2):
                    for m in range(MT):
                        k = 2 * n + q
                        last = turn(bank[2 + n % 2][:, q * S + m * P:q * S + (m + 1) * P], x_sb[:, m, k * P:(k + 1) * P])
                last.then_inc(N["x_turned"].sem, 1)
            pe.wait_ge(p_in.sem, 16 * 6)
            for n, (at, r) in enumerate(((0, 96), (96, 96), (192, 96), (288, 48), (336, 3 * KT))):
                last = t_.transpose(bank[0][:, at:at + r], rows[0:r, n, :], ident[0:r, 0:r])
            last.then_inc(N["rows_turned"].sem, 1)
            pe.wait_ge(N["masks_made"].sem, 1)
            pe.wait_ge(N["c_made"].sem, 1)
            for n in range(NMOD_FIRST):
                pe.wait_ge(N["macc_first"].sem, n + 1)
                for b in range(BPC):
                    at = KT + n * BPC + b
                    last = mm(bank[1][:, at:at + 1], macc[:, n % 2, b * P:(b + 1) * P], ones[:, 0:1])
                last.then_inc(N["mcol_first"].sem, 1)
            pe.wait_ge(ws_in.sem, 32)
            pe.wait_ge(N["x_copied"].sem, 8)
            for k in range(KT):
                pe.wait_ge(N["u_odd" if k % 2 else "u_even"].sem, k // 2 + 1)
                for m in range(MT):
                    last = mm(bank[2 + m][:, 0:NSM], uT[:, k, m * P:(m + 1) * P], ws[:, k, :], k == 0, k == KT - 1)
            last.then_inc(N["small_done"].sem, 1)
            pe.wait_ge(N["logs_made"].sem, 1)
            for m in range(MT):
                mm(bank[1][:, m * VH:(m + 1) * VH], chunk_upper[:, :], sm2[:, m, VH:2 * VH])
                mm(bank[1][:, (MT + m) * VH:(MT + m + 1) * VH], chunk_ones[:, :], sm2[:, m, VH:2 * VH])
                for h in range(2):
                    mm(bank[2][:, (2 * m + h) * VH:(2 * m + h + 1) * VH], half_rows[:, h, :], sm2[:, m, VH:2 * VH])
            mm(bank[3][:, 0:FH], upper[:, :], sm2[:, 0, 2 * VH:NSM])
            mm(bank[3][:, FH:2 * FH], ones[:, :], sm2[:, 0, 2 * VH:NSM], True, False)
            mm(bank[3][:, FH:2 * FH], upper[:, :], sm2[:, 1, 2 * VH:NSM], False, True).then_inc(N["sums_done"].sem, 1)
            pe.wait_ge(N["u_lo_made"].sem, KT // 2)

            with pe.Fori(0, NCH) as i:
                count = [0]
                next_slot = slots(i, MAIN_UNITS, 0, count, lambda job, s: (u_hi, u_lo))

                def wait(name, k):
                    pe.wait_ge(N[name].sem, N[name].value(i, k))

                def until(job):
                    while count[0] < (job + 1) * KT:
                        next_slot()

                def wait_taken(job):
                    pe.wait_ge(acc_free[job % 2].sem, i * (len(MAIN_JOBS) // 2) + (job // 2 + 2))

                def turn_stage(b0, name, k):
                    for b in range(BPC):
                        for m in range(MT):
                            last = turn(bank[b0 + b // 2][:, (b % 2) * S + m * P:(b % 2) * S + (m + 1) * P],
                                        stage[:, m, b * P:(b + 1) * P])
                    last.then_inc(N[name].sem, 1)

                def mod_columns(n):
                    wait("macc_ready", n + 1)
                    for b in range(BPC):
                        last = mm(bank[MOD_BANK[n]][:, b:b + 1], macc[:, n % 2, b * P:(b + 1) * P], ones[:, 0:1])
                    last.then_inc(N["mcol_done"].sem, 1)

                fence(pe, "pe", i, 1, None, lambda: until(J_GQ))
                for k, job in enumerate((J_GQ, J_GK, J_GV)):
                    until(job)
                    next_slot(2)
                    wait_taken(job)
                    if k == 2:
                        wait("rn_made", 1)
                    turn_stage(2 * (k % 2), "turned", k + 1)
                    next_slot()
                    if k == 1:
                        next_slot(9)
                        wait("sq_made", 1)
                        wait("conv_made", 2)
                        for n in range(4):
                            last = mm(bank[n][:, :], ones[:, :], norm_tmp[n])
                        last.then_inc(N["ssq_done"].sem, 1)
                next_slot(8)
                wait("qk_made", 1)
                wait("conv_made", 3)
                wait("silu_made", 3)
                for b in range(BPC):
                    for m in range(MT):
                        last = turn(bank[m][:, b * P:(b + 1) * P], KC[:, b, m * P:(m + 1) * P])
                last.then_inc(N["tok_done"].sem, 1)
                for b in range(BPC):
                    for m in range(MT):
                        last = turn(bank[2 + m][:, b * P:(b + 1) * P], VC[:, b, m * P:(m + 1) * P])
                last.then_inc(N["tok_done"].sem, 1)
                next_slot(3)
                wait("k_tok_in", 1)
                mod_columns(0)
                next_slot()

                def delta_pair(pair):
                    wait("mod_made", pair + 1)
                    fence(pe, "pe", i, 2 + pair, None, next_slot)
                    for e in range(2):
                        k = 2 * pair + e
                        for q in range(4):
                            t, r = divmod(q, 2)
                            g_col = cur[:, 0, t, 2 * k + r:2 * k + r + 1].broadcast_to([P, P])
                            last = turn(bank[2 + e][:, q * P:(q + 1) * P], g_col)
                        last.then_inc(N["gb_done"].sem, 1)
                        for t in range(MT):
                            ts_ = slice(t * P, (t + 1) * P)
                            mm(bank[e][:, t * P:(t + 1) * P], KC[:, k, ts_], KC[:, k, ts_])
                            last = mm(bank[e][:, (MT + t) * P:(MT + t + 1) * P], KC[:, k, ts_], QC[:, k, ts_])
                        last.then_inc(N["kk_done"].sem, 1)
                    next_slot(3)
                    for e in range(2):
                        k = 2 * pair + e
                        wait("low_made", k + 1)
                        wait("it_made", k + 1)
                        for q in range(4):
                            last = turn(bank[e][:, q * P:(q + 1) * P], X[e]["KB"][:, q, :])
                        last.then_inc(N["low_turned"].sem, 1)
                    next_slot(5)
                    for e in range(2):
                        k = 2 * pair + e
                        wait("t1_made", k + 1)
                        for q in range(4):
                            last = turn(bank[2 + e][:, q * P:(q + 1) * P], X[e]["T"][:, q, :])
                        last.then_inc(N["t1_turned"].sem, 1)
                    next_slot()
                    for l in range(LEVELS):
                        for e in range(2):
                            k = 2 * pair + e
                            n = pair * 2 * LEVELS + 2 * l + e + 1
                            x_ = X[e]
                            wait("b_made", pair * 2 * (LEVELS + 1) + 2 * (l + 1) + e + 1)
                            if l == 0:
                                wait("tt1_made", k + 1)
                                wait("l_made", k + 1)
                            else:
                                wait("t_made", pair * 2 * (LEVELS - 1) + 2 * (l - 1) + e + 1)
                                wait("tt_made", n - 2)
                            for q in range(4):
                                last = mm(bank[e][:, q * P:(q + 1) * P], x_["B"][:, q, :], x_["TT"][:, q, :])
                            last.then_inc(N["v_done"].sem, 1)
                        next_slot()
                        for e in range(2):
                            n = pair * 2 * LEVELS + 2 * l + e + 1
                            x_ = X[e]
                            wait("v_made", n)
                            for q in range(4):
                                last = mm(d_half(e, 0, q, l), x_["T"][:, q, :], halves_of(x_["V"], l, 1)[:, q])
                            if l < LEVELS - 1:
                                for q in range(4):
                                    last = mm(d_half(e, 1, q, l), x_["V"][:, q, :], halves_of(x_["T"], l, 0)[:, q])
                            last.then_inc(N["d_done"].sem, 1)
                        next_slot()
                    wait("tt_made", (pair + 1) * 2 * LEVELS)
                    for e in range(2):
                        k = 2 * pair + e
                        x_ = X[e]
                        wait("kb_made", k + 1)
                        for q in range(4):
                            last = mm(bank[e][:, q * P:(q + 1) * P], x_["KB"][:, q, :], x_["TT"][:, q, :])
                        last.then_inc(N["wt_done"].sem, 1)
                        wait("vb_made", k + 1)
                        for q in range(4):
                            last = mm(bank[2 + e][:, q * DV:(q + 1) * DV], x_["TT"][:, q, :], x_["VB"][:, q, :])
                        last.then_inc(N["u_done"].sem, 1)
                    next_slot(3)
                    for j in range(NCK):
                        t, h = divmod(j, 2)
                        rw = slice(CH * h, CH * h + CH)
                        first = pair * 2 * NCK + 2 * j + 1
                        for e in range(2):
                            k = 2 * pair + e
                            x_ = X[e]
                            if j == 0:
                                wait("wt_made", k + 1)
                                wait("uu_made", k + 1)
                                wait("s_zero", k + 1)
                            else:
                                wait("s_made", first + e - 2)
                                wait("o_made", first + e - 2)
                                wait("o1_made", first + e - 2)
                            for r in range(2):
                                last = mm(bank[e][rw, r * DV:(r + 1) * DV], x_["WT"][:, 2 * t + r, rw], x_["ST"][:, r * DV:(r + 1) * DV])
                            last.then_inc(N["ws_done"].sem, 1)
                            mm(bank[2 + e][rw, P:2 * P], QC[:, k, j * CH:(j + 1) * CH], x_["ST"][:, :]).then_inc(N["qs_done"].sem, 1)
                        next_slot()
                        for e in range(2):
                            k = 2 * pair + e
                            x_ = X[e]
                            wait("vs_made", first + e)
                            wait("o1_made", first + e)
                            if j == 0:
                                wait("it_masked", k + 1)
                            mm(bank[2 + e][:, 2 * P:3 * P], ktok[rw, t, k * P:(k + 1) * P], x_["VS"][rw, :]).then_inc(N["su_done"].sem, 1)
                            for r in range(2):
                                last = mm(bank[e][rw, P + r * DV:P + (r + 1) * DV], x_["IT"][rw, 2 * t + r, rw], x_["VN"][rw, r * DV:(r + 1) * DV])
                            last.then_inc(N["in_done"].sem, 1)
                        next_slot()

                delta_pair(0)
                for n, job in enumerate((J_FQ, J_FK)):
                    until(job)
                    next_slot()
                    wait_taken(job)
                    if n == 0:
                        wait("o_made", 2 * NCK)
                        wait("s_made", 2 * NCK)
                    turn_stage(2 * n, "f_turned", n + 1)
                    if n == 1:
                        wait("f_made", 1)
                        mod_columns(1)
                    next_slot()
                delta_pair(1)
                fence(pe, "pe", i, 4, None, lambda: next_slot(2))
                for f in range(KPC):
                    for t in range(MT):
                        last = turn(bank[2 + f // 2][:, (f % 2) * S + t * P:(f % 2) * S + (t + 1) * P],
                                    cur_f[:, t, f:f + 1].broadcast_to([P, P]))
                last.then_inc(N["cum_done"].sem, 1)
                next_slot(4)
                wait("bias_made", 1)
                for f in range(KPC):
                    mm(bank[f][:, 0:P], FQ[:, f, 0:P], FK[:, f, 0:P])
                    last = mm(bank[f][:, P:3 * P], FQ[:, f, P:2 * P], FK[:, f, 0:2 * P])
                last.then_inc(N["scores_done"].sem, 1)
                next_slot(4)
                wait("scored", 1)
                wait("yb_tok", MT)
                for b in range(BPC):
                    for m in range(MT):
                        last = turn(bank[b // 2][:, (b % 2) * S + m * P:(b % 2) * S + (m + 1) * P], vtok[:, m, b * P:(b + 1) * P])
                last.then_inc(N["yb_turned"].sem, 1)
                mod_columns(2)
                next_slot(4)
                wait("yb_made", 1)
                wait("prob_made", 1)
                wait("mod_made", 3)
                for f in range(KPC):
                    for n in range(3):
                        last = turn(bank[f][:, n * P:(n + 1) * P], SC[:, f, n * P:(n + 1) * P])
                last.then_inc(N["prob_turned"].sem, 1)
                next_slot(2)
                wait("probT_made", 1)
                for f in range(KPC):
                    fs = slice(f * P, (f + 1) * P)
                    mm(bank[f][:, 0:P], FV[:, 0, fs], PT[:, f, 0:P])
                    mm(bank[f][:, P:2 * P], FV[:, 0, fs], PT[:, f, P:2 * P], True, False)
                    last = mm(bank[f][:, P:2 * P], FV[:, 1, fs], PT[:, f, 2 * P:3 * P], False, True)
                last.then_inc(N["yc_done"].sem, 1)
                next_slot(2)
                wait_taken(J_CC)
                wait("yc_made", 1)
                mod_columns(3)
                turn_stage(0, "c_turned", 1)
                for n, job in ((1, J_CH), (2, J_CB)):
                    until(job)
                    next_slot(2)
                    wait_taken(job)
                    if n == 2:
                        wait("cc_made", 1)
                    else:
                        wait("mod_made", 4)
                    turn_stage(2 * (n % 2), "c_turned", n + 1)
                    next_slot()
                assert count[0] >= 2 * MAIN_UNITS
            pe.sem_inc(met["pe"].sem, 1)

            for b in range(3):
                with pe.Fori(0, NCH) as i:
                    count = [0]

                    def merge_left(job, s):
                        if job == 0:
                            return u_hi, u_lo
                        if s % 4 == 0:
                            pe.wait_ge(N["y_lo"].sem, 4 * b + (s - KT) // 4 + 1)
                        return z_hi, z_lo

                    next_slot = slots(i, 2 * UPJ, J_MERGE * UPJ + b * 2 * UPJ * NCH, count, merge_left)
                    for _ in range(4 * UPJ):
                        next_slot()
            for n in range(8):
                pe.wait_ge(N["merged_made"].sem, 2 * NCH + n // 2 + 1)
                if n >= 4:
                    pe.wait_ge(N["z_lo_made"].sem, n - 3)
                for q in range(2):
                    k = 2 * n + q
                    for m in range(MT):
                        last = turn(bank[n % 4][:, q * S + m * P:q * S + (m + 1) * P], merged[:, m, k * P:(k + 1) * P])
                last.then_inc(N["z_turned"].sem, 1)

            def gate_rows(which, at):
                for n in range(NCH):
                    if which:
                        pe.wait_ge(N["gate_made"].sem, NCH)
                    for b in range(BPC):
                        k = at + n * BPC + b
                        last = mm(bank[n][:, b * P:(b + 1) * P], mod[:, k:k + 1].broadcast_to([P, P]), ident[:, :])
                    last.then_inc(N["gate_done"].sem, 1)

            pe.wait_ge(N["z_lo_made"].sem, 8)
            gate_rows(0, 2 * KT)
            with pe.Fori(0, NCH // 2) as i:
                count = [0]
                next_slot = slots(i, 2 * UPJ, J_OUT * UPJ, count, lambda job, s: (z_hi, z_lo))
                for _ in range(4 * UPJ):
                    next_slot()
            gate_rows(1, 5 * KT)
            pe.wait_ge(N["gate_made"].sem, 2 * NCH)
            for k in range(KT):
                pe.wait_ge(N["xhat_made"].sem, k // BPC + 1)
                if k >= 4:
                    pe.wait_ge(N["u2_odd" if k % 2 else "u2_even"].sem, k // 2 - 1)
                for m in range(MT):
                    last = turn(bank[k % 4][:, m * P:(m + 1) * P], x1[:, m, k * P:(k + 1) * P])
                last.then_inc(N["xhat_turned"].sem, 1)
            with pe.Fori(0, FFQ) as i:
                count = [0]

                def ff_left(job, s):
                    if job == 0 and s % 2 == 0:
                        pe.wait_ge(N["u2_lo"].sem, s // 2 + 1)
                    if job < NCH:
                        return u_hi, u_lo
                    if job == NCH and s % 2 == 0:
                        pe.wait_ge(N["h_lo"].sem, N["h_lo"].value(i, (s - NCH * KT) // 2 + 1))
                    return z_hi, z_lo

                next_slot = slots(i, FF_JOBS * UPJ, J_FF * UPJ, count, ff_left)
                for j in range(FF_JOBS):
                    while count[0] < (j + 1) * KT:
                        next_slot()
                    if j < NCH:
                        next_slot(2)
                        pe.wait_ge(N["squared"].sem, N["squared"].value(i, j + 1))
                        for b in range(BPC):
                            for m in range(MT):
                                last = turn(bank[2 * (j % 2) + b // 2][:, (b % 2) * S + m * P:(b % 2) * S + (m + 1) * P],
                                            stage[:, m, b * P:(b + 1) * P])
                        last.then_inc(N["h_turned"].sem, 1)


_INPUTS = ["x", "c", "w_ada", "b_ada", "w_in", "conv_w", "gdn_conv_w", "gdn_a_log", "gdn_dt_bias",
           "gdn_norm_w", "fox_f_bias", "w_branch_a", "w_branch_b", "w_branch_c", "w_o", "ln1_g", "ln1_b",
           "w_ff1", "w_ff2", "ln2_g", "ln2_b"]


def kernel(**inputs):
    import numpy as np
    import concourse.bacc as bacc
    from concourse.bass_utils import run_bass_kernel_spmd

    nc = bacc.Bacc("TRN2", target_bir_lowering=False, num_devices=1)
    arrays, args = {}, []
    for name in _INPUTS:
        arrays[f"in_{name}"] = np.ascontiguousarray(inputs[name])
        args.append(nc.dram_tensor(f"in_{name}", arrays[f"in_{name}"].shape, F32, kind="ExternalInput").ap())
    out = nc.dram_tensor("out_dram", (1, S, D), F32, kind="ExternalOutput").ap()
    layer_program(nc, *args, out)
    return run_bass_kernel_spmd(nc, [arrays], core_ids=[0]).results[0]["out_dram"]
```
